# Optimizing a Trainium2 kernel written in Bass

```python
import math
import jax, jax.numpy as jnp
from jax import lax
import numpy as np

D_MODEL = 1024
BATCH = 1
SEQ = 512
DEPTH = 2

N_POOL_LAYERS = DEPTH // 2
N_ATTN_LAYERS = DEPTH - N_POOL_LAYERS
POOL_WINDOWS = (2, 4, 8, 16)
N_POOL_GROUPS = len(POOL_WINDOWS)
POOL_GROUP_DIM = D_MODEL // N_POOL_GROUPS
BRANCHES = ((128, 1), (512, 4), (2048, 16))
N_BRANCHES = len(BRANCHES)
HEAD_DIM = 64
N_HEADS = D_MODEL // HEAD_DIM
D_ATTN = N_HEADS * HEAD_DIM
ATTN_BLOCK = 128
D_FF = 2816
CONV_WIDTH = 3
EPS = 1e-6
ADA_SCALE = 0.5


def _rmsnorm(x, g):
    x32 = x.astype(jnp.float32)
    y = x32 * lax.rsqrt(jnp.mean(x32 * x32, axis=-1, keepdims=True) + EPS)
    return (y * g.astype(jnp.float32)).astype(x.dtype)

def _modulate(h, shift, scale):
    return h * (1 + scale[:, None, :]) + shift[:, None, :]

def _alibi_slopes(n):
    def pow2(m):
        start = 2.0 ** (-(2.0 ** -(math.log2(m) - 3)))
        return [start ** (i + 1) for i in range(m)]
    if math.log2(n).is_integer():
        s = pow2(n)
    else:
        c = 2 ** math.floor(math.log2(n))
        s = pow2(c) + pow2(2 * c)[0::2][: n - c]
    s = np.asarray(s, dtype=np.float32)
    return -np.sort(-s)

def _pool_mixer(h, w_in, w_grp, scale, w_out):
    b, s, _ = h.shape
    u = (h @ w_in).reshape(b, s, N_POOL_GROUPS, POOL_GROUP_DIM)
    u32 = u.astype(jnp.float32)
    csum = jnp.cumsum(u32, axis=1)
    t = jnp.arange(s)
    outs = []
    for g, w in enumerate(POOL_WINDOWS):
        cs = csum[:, :, g]
        lag = jnp.pad(cs, ((0, 0), (w, 0), (0, 0)))[:, :s]
        count = jnp.minimum(t + 1, w).astype(jnp.float32)[None, :, None]
        pooled = (cs - lag) / count - u32[:, :, g]
        outs.append(jnp.einsum('bsc,cd->bsd', pooled.astype(h.dtype), w_grp[g]))
    y = jnp.concatenate(outs, axis=-1) * scale
    return y @ w_out

def _causal_dwconv(a, w, bias):
    s = a.shape[1]
    ap = jnp.pad(a, ((0, 0), (CONV_WIDTH - 1, 0), (0, 0)))
    y = bias
    for k in range(CONV_WIDTH):
        y = y + ap[:, k:k + s] * w[k]
    return y

def _conv_ffn(h, w_up, conv_w, conv_b, w_down):
    a, v = jnp.split(h @ w_up, 2, axis=-1)
    a = _causal_dwconv(a, conv_w, conv_b)
    return (jax.nn.silu(a) * v) @ w_down

def _dilated_branch(q, k, v, window, dilation, slopes):
    b, s, h, dh = q.shape
    n_steps = window // dilation
    blk = max(ATTN_BLOCK, n_steps)
    sub_len = s // dilation
    nb = -(-sub_len // blk)
    sub_pad = nb * blk

    def to_sub(t):
        t = t.reshape(b, sub_len, dilation, h, dh).transpose(0, 2, 1, 3, 4).reshape(b * dilation, sub_len, h, dh)
        return jnp.pad(t, ((0, 0), (0, sub_pad - sub_len), (0, 0), (0, 0)))

    def with_prev(t):
        tb = t.reshape(-1, nb, blk, h, dh)
        prev = jnp.pad(tb, ((0, 0), (1, 0), (0, 0), (0, 0), (0, 0)))[:, :nb]
        return jnp.concatenate([prev, tb], axis=2)

    qb = to_sub(q).reshape(-1, nb, blk, h, dh)
    kb = with_prev(to_sub(k))
    vb = with_prev(to_sub(v))

    scores = jnp.einsum('bnqhd,bnkhd->bnhqk', qb, kb).astype(jnp.float32) * (dh ** -0.5)
    qi = jnp.arange(blk)[:, None] + blk
    ki = jnp.arange(2 * blk)[None, :]
    delta = qi - ki
    key_idx = jnp.arange(nb)[:, None] * blk + jnp.arange(2 * blk)[None, :] - blk
    valid = ((delta >= 0) & (delta <= n_steps))[None] & (key_idx >= 0)[:, None, :]
    bias = -slopes[:, None, None] * (delta * dilation).astype(jnp.float32)[None]
    scores = jnp.where(valid[None, :, None], scores + bias[None, None], -jnp.inf)
    lse = jax.nn.logsumexp(scores, axis=-1)
    p = jnp.exp(scores - lse[..., None])
    out = jnp.einsum('bnhqk,bnkhd->bnqhd', p.astype(v.dtype), vb)

    out = out.reshape(b, dilation, sub_pad, h, dh)[:, :, :sub_len]
    out = out.transpose(0, 2, 1, 3, 4).reshape(b, s, h, dh)
    lse = lse.transpose(0, 1, 3, 2).reshape(b, dilation, sub_pad, h)[:, :, :sub_len]
    lse = lse.transpose(0, 2, 1, 3).reshape(b, s, h)
    return out, lse

def _dilated_attention(h, kv, w_q, w_o, slopes):
    b, s, _ = h.shape
    q = (h @ w_q).reshape(b, s, N_BRANCHES, N_HEADS, HEAD_DIM)
    outs, lses = [], []
    for g, (window, dil) in enumerate(BRANCHES):
        o, l = _dilated_branch(q[:, :, g], kv[:, :, 0, g], kv[:, :, 1, g], window, dil, slopes[g])
        outs.append(o)
        lses.append(l)
    wts = jax.nn.softmax(jnp.stack(lses, axis=0), axis=0)
    o = jnp.sum(wts[..., None] * jnp.stack(outs, axis=0).astype(jnp.float32), axis=0)
    return o.reshape(b, s, D_ATTN).astype(h.dtype) @ w_o

def first_inputs(seed: int = 0) -> dict:
    key = jax.random.key(seed)
    ks = jax.random.split(key, 24)

    def nrm(k, shape, scale):
        return jax.random.normal(k, shape, jnp.float32) * scale

    D, F, G = D_MODEL, D_FF, N_BRANCHES
    return {
        "x": nrm(ks[0], (BATCH, SEQ, D), 1.0),
        "c": nrm(ks[1], (BATCH, D), 1.0),
        "ada_w": nrm(ks[2], (DEPTH, D, 6 * D), ADA_SCALE * D ** -0.5),
        "ada_b": nrm(ks[3], (DEPTH, 6 * D), 0.02),
        "norm1_g": 1.0 + nrm(ks[4], (DEPTH, D), 0.05),
        "norm2_g": 1.0 + nrm(ks[5], (DEPTH, D), 0.05),
        "pool_w_in": nrm(ks[6], (N_POOL_LAYERS, D, D), D ** -0.5),
        "pool_w_grp": nrm(ks[7], (N_POOL_LAYERS, N_POOL_GROUPS, POOL_GROUP_DIM, POOL_GROUP_DIM), POOL_GROUP_DIM ** -0.5),
        "pool_scale": 1.0 + nrm(ks[8], (N_POOL_LAYERS, D), 0.1),
        "pool_w_out": nrm(ks[9], (N_POOL_LAYERS, D, D), D ** -0.5),
        "kv_norm_g": 1.0 + nrm(ks[10], (D,), 0.05),
        "kv_ada_w": nrm(ks[11], (D, 2 * D), ADA_SCALE * D ** -0.5),
        "kv_ada_b": nrm(ks[12], (2 * D,), 0.02),
        "w_kv": nrm(ks[13], (D, 2 * G * D_ATTN), D ** -0.5),
        "attn_w_q": nrm(ks[14], (N_ATTN_LAYERS, D, G * D_ATTN), D ** -0.5),
        "attn_w_o": nrm(ks[15], (N_ATTN_LAYERS, D_ATTN, D), D_ATTN ** -0.5),
        "ffn_w_up": nrm(ks[16], (DEPTH, D, 2 * F), D ** -0.5),
        "ffn_conv_w": nrm(ks[17], (DEPTH, CONV_WIDTH, F), CONV_WIDTH ** -0.5),
        "ffn_conv_b": nrm(ks[18], (DEPTH, F), 0.02),
        "ffn_w_down": nrm(ks[19], (DEPTH, F, D), F ** -0.5),
        "final_g": 1.0 + nrm(ks[20], (D,), 0.05),
    }

def first_block(x, c, ada_w, ada_b, norm1_g, norm2_g, pool_w_in, pool_w_grp, pool_scale, pool_w_out,
              kv_norm_g, kv_ada_w, kv_ada_b, w_kv, attn_w_q, attn_w_o,
              ffn_w_up, ffn_conv_w, ffn_conv_b, ffn_w_down, final_g):
    b, s, _ = x.shape
    cond = jax.nn.silu(c)
    slopes = jnp.asarray(_alibi_slopes(N_BRANCHES * N_HEADS)).reshape(N_BRANCHES, N_HEADS)
    kv = None
    for layer in range(DEPTH):
        mod = cond @ ada_w[layer] + ada_b[layer]
        sh1, sc1, g1, sh2, sc2, g2 = jnp.split(mod, 6, axis=-1)
        h = _modulate(_rmsnorm(x, norm1_g[layer]), sh1, sc1)
        if layer < N_POOL_LAYERS:
            y = _pool_mixer(h, pool_w_in[layer], pool_w_grp[layer], pool_scale[layer], pool_w_out[layer])
        else:
            if layer == N_POOL_LAYERS:
                kv_shift, kv_scale = jnp.split(cond @ kv_ada_w + kv_ada_b, 2, axis=-1)
                hkv = _modulate(_rmsnorm(x, kv_norm_g), kv_shift, kv_scale)
                kv = (hkv @ w_kv).reshape(b, s, 2, N_BRANCHES, N_HEADS, HEAD_DIM)
            j = layer - N_POOL_LAYERS
            y = _dilated_attention(h, kv, attn_w_q[j], attn_w_o[j], slopes)
        x = x + g1[:, None, :] * y
        h = _modulate(_rmsnorm(x, norm2_g[layer]), sh2, sc2)
        x = x + g2[:, None, :] * _conv_ffn(h, ffn_w_up[layer], ffn_conv_w[layer], ffn_conv_b[layer], ffn_w_down[layer])
    return _rmsnorm(x, final_g)


CHUNK = 64
HEAD_DIM_2 = 128
MIX_WIDTH = D_MODEL
RET_WIDTH = MIX_WIDTH // 2
SB_WIDTH = MIX_WIDTH - RET_WIDTH
N_RET_HEADS = RET_WIDTH // HEAD_DIM_2
N_SB_HEADS = SB_WIDTH // HEAD_DIM_2
D_FF_2 = ((8 * D_MODEL // 3 + 255) // 256) * 256
SB_BLOCK = 128
ROPE_BASE = 10000.0
IN_WIDTHS = (RET_WIDTH, RET_WIDTH, RET_WIDTH, RET_WIDTH, SB_WIDTH, SB_WIDTH, SB_WIDTH)
IN_WIDTH = sum(IN_WIDTHS)
IN_SPLITS = tuple(int(c) for c in np.cumsum(IN_WIDTHS)[:-1])


def rms_norm(x, g):
    xf = x.astype(jnp.float32)
    y = xf * lax.rsqrt(jnp.mean(xf * xf, axis=-1, keepdims=True) + EPS)
    return (y * g.astype(jnp.float32)).astype(x.dtype)

def to_heads(t, n_heads):
    b, s, _ = t.shape
    return t.reshape(b, s, n_heads, HEAD_DIM_2).transpose(0, 2, 1, 3)

def from_heads(t):
    b, h, s, d = t.shape
    return t.transpose(0, 2, 1, 3).reshape(b, s, h * d)

def head_group_norm(x, g):
    h, d = x.shape[1], x.shape[3]
    xf = x.astype(jnp.float32)
    mu = jnp.mean(xf, axis=-1, keepdims=True)
    var = jnp.mean(jnp.square(xf - mu), axis=-1, keepdims=True)
    y = (xf - mu) * lax.rsqrt(var + EPS) * g.astype(jnp.float32).reshape(h, 1, d)
    return y.astype(x.dtype)

def head_rms_norm(x, g):
    h, d = x.shape[1], x.shape[3]
    xf = x.astype(jnp.float32)
    y = xf * lax.rsqrt(jnp.mean(xf * xf, axis=-1, keepdims=True) + EPS)
    return (y * g.astype(jnp.float32).reshape(h, 1, d)).astype(x.dtype)

def apply_rotary(x):
    s, d = x.shape[2], x.shape[3]
    inv_freq = 1.0 / (ROPE_BASE ** (jnp.arange(0, d, 2, dtype=jnp.float32) / d))
    ang = jnp.arange(s, dtype=jnp.float32)[:, None] * inv_freq[None, :]
    cos = jnp.cos(ang).astype(x.dtype)
    sin = jnp.sin(ang).astype(x.dtype)
    x1, x2 = x[..., : d // 2], x[..., d // 2:]
    return jnp.concatenate([x1 * cos - x2 * sin, x1 * sin + x2 * cos], axis=-1)

def chunk_retention(q, k, v):
    b, h, s, d = q.shape
    c = CHUNK
    n = s // c
    dt = q.dtype
    log_g = jnp.log1p(-jnp.exp2(-5.0 - jnp.arange(h, dtype=jnp.float32)))
    i = jnp.arange(c, dtype=jnp.float32)
    intra_decay = jnp.exp(log_g[:, None, None] * jnp.abs(i[:, None] - i[None, :])).astype(dt)
    q_decay = jnp.exp(log_g[:, None] * (i + 1.0)).astype(dt)[..., None]
    k_decay = jnp.exp(log_g[:, None] * (c - 1.0 - i)).astype(dt)[..., None]
    chunk_decay = jnp.exp(log_g * c).astype(dt)[None, :, None, None]
    k = k * (d ** -0.5)
    qc = q.reshape(b, h, n, c, d)
    kc = k.reshape(b, h, n, c, d)
    vc = v.reshape(b, h, n, c, v.shape[-1])
    scores = jnp.einsum('bhnid,bhnjd->bhnij', qc, kc) * intra_decay[:, None]
    intra = jnp.einsum('bhnij,bhnje->bhnie', scores, vc)

    def step(state, inp):
        q_n, k_n, v_n = inp
        cross = jnp.einsum('bhid,bhde->bhie', q_n * q_decay, state)
        state = state * chunk_decay + jnp.einsum('bhjd,bhje->bhde', k_n * k_decay, v_n)
        return state, cross

    init = jnp.zeros((b, h, d, v.shape[-1]), dtype=intra.dtype)
    xs = (jnp.moveaxis(qc, 2, 0), jnp.moveaxis(kc, 2, 0), jnp.moveaxis(vc, 2, 0))
    _, cross = lax.scan(step, init, xs)
    out = intra + jnp.moveaxis(cross, 0, 2)
    return out.reshape(b, h, s, v.shape[-1])

def stick_breaking(q, k, v):
    s, d = q.shape[2], q.shape[3]
    scale = d ** -0.5
    outs = []
    for start in range(0, s, SB_BLOCK):
        end = start + SB_BLOCK
        qb = q[:, :, start:end]
        kb = k[:, :, :end]
        vb = v[:, :, :end]
        z = jnp.einsum('bhtd,bhsd->bhts', qb, kb).astype(jnp.float32) * scale
        t_pos = jnp.arange(start, end)[:, None]
        s_pos = jnp.arange(end)[None, :]
        valid = s_pos < t_pos
        log_keep = jnp.where(valid, jax.nn.log_sigmoid(-z), 0.0)
        later = lax.cumsum(log_keep, axis=3, reverse=True) - log_keep
        w = jnp.where(valid, jnp.exp(jax.nn.log_sigmoid(z) + later), 0.0)
        outs.append(jnp.einsum('bhts,bhse->bhte', w.astype(v.dtype), vb))
    return jnp.concatenate(outs, axis=2)

def second_inputs(seed: int = 0) -> dict:
    key = jax.random.key(seed)
    ks = jax.random.split(key, 12)
    f32 = jnp.float32

    def gain(k, shape):
        return (1.0 + 0.02 * jax.random.normal(k, shape, f32)).astype(f32)

    return {
        "x": jax.random.normal(ks[0], (BATCH, SEQ, D_MODEL), f32),
        "norm1_g": gain(ks[1], (DEPTH, D_MODEL)),
        "w_in": jax.random.normal(ks[2], (DEPTH, D_MODEL, IN_WIDTH), f32) * D_MODEL ** -0.5,
        "ret_norm_g": gain(ks[3], (DEPTH, RET_WIDTH)),
        "sb_norm_g": gain(ks[4], (DEPTH, SB_WIDTH)),
        "w_out": jax.random.normal(ks[5], (DEPTH, MIX_WIDTH, D_MODEL), f32) * MIX_WIDTH ** -0.5,
        "norm2_g": gain(ks[6], (DEPTH, D_MODEL)),
        "w_gate": jax.random.normal(ks[7], (DEPTH, D_MODEL, D_FF_2), f32) * D_MODEL ** -0.5,
        "w_up": jax.random.normal(ks[8], (DEPTH, D_MODEL, D_FF_2), f32) * D_MODEL ** -0.5,
        "w_down": jax.random.normal(ks[9], (DEPTH, D_FF_2, D_MODEL), f32) * D_FF_2 ** -0.5,
        "final_g": gain(ks[10], (D_MODEL,)),
    }

def second_block(x, norm1_g, w_in, ret_norm_g, sb_norm_g, w_out, norm2_g, w_gate, w_up, w_down, final_g):
    for l in range(DEPTH):
        h = rms_norm(x, norm1_g[l])
        proj = h @ w_in[l]
        rq, rk, rv, rg, sq, sk, sv = jnp.split(proj, IN_SPLITS, axis=-1)
        ret = chunk_retention(apply_rotary(to_heads(rq, N_RET_HEADS)),
                              apply_rotary(to_heads(rk, N_RET_HEADS)),
                              to_heads(rv, N_RET_HEADS))
        ret = from_heads(head_group_norm(ret, ret_norm_g[l])) * jax.nn.silu(rg)
        sb = stick_breaking(to_heads(sq, N_SB_HEADS), to_heads(sk, N_SB_HEADS), to_heads(sv, N_SB_HEADS))
        sb = from_heads(head_rms_norm(sb, sb_norm_g[l]))
        x = x + jnp.concatenate([ret, sb], axis=-1) @ w_out[l]
        h = rms_norm(x, norm2_g[l])
        x = x + (jax.nn.silu(h @ w_gate[l]) * (h @ w_up[l])) @ w_down[l]
    return rms_norm(x, final_g)


def setup_inputs(seed=0):
    out = dict(first_inputs(seed))
    for name, value in second_inputs(seed + 1).items():
        if name != "x":
            out[name + "_2"] = value
    return out


def reference(
    x, c, ada_w, ada_b, norm1_g, norm2_g, pool_w_in, pool_w_grp, pool_scale, pool_w_out,
    kv_norm_g, kv_ada_w, kv_ada_b, w_kv, attn_w_q, attn_w_o, ffn_w_up, ffn_conv_w, ffn_conv_b,
    ffn_w_down, final_g, norm1_g_2, w_in_2, ret_norm_g_2, sb_norm_g_2, w_out_2, norm2_g_2,
    w_gate_2, w_up_2, w_down_2, final_g_2,
):
    x = first_block(
        x, c, ada_w, ada_b, norm1_g, norm2_g, pool_w_in, pool_w_grp, pool_scale, pool_w_out,
        kv_norm_g, kv_ada_w, kv_ada_b, w_kv, attn_w_q, attn_w_o, ffn_w_up, ffn_conv_w,
        ffn_conv_b, ffn_w_down, final_g,
    )
    return second_block(
        x, norm1_g_2, w_in_2, ret_norm_g_2, sb_norm_g_2, w_out_2, norm2_g_2, w_gate_2, w_up_2,
        w_down_2, final_g_2,
    )


_drawn_inputs = setup_inputs


def setup_inputs(seed=0):
    import zlib

    import numpy as np

    out = dict(_drawn_inputs(seed))
    spreads = {}
    factors = {'kv_norm_g': 4.282,
     'kv_ada_b': 5.988,
     'ffn_conv_b': 6.619,
     'ret_norm_g_2': 5.876,
     'sb_norm_g_2': 3.352,
     'norm2_g_2': 3.292,
     'final_g_2': 2.865}
    for name, (base, spread) in spreads.items():
        noise = np.random.default_rng([zlib.crc32(name.encode()), seed]).standard_normal(out[name].shape)
        drawn = base * np.exp(spread * noise) if base else spread * noise
        out[name] = __import__('jax').numpy.asarray(drawn.astype(out[name].dtype))
    for name, factor in factors.items():
        out[name] = (out[name] * factor).astype(out[name].dtype)
    return out
```

```python
import math
from contextlib import ExitStack

import numpy as np
import concourse.bass as bass
from concourse import mybir

F32 = mybir.dt.float32
F32R = mybir.dt.float32r
ALU = mybir.AluOpType
ACT = mybir.ActivationFunctionType
AX_X = mybir.AxisListType.X

D, S, F, KC, FC, HC = 1024, 512, 2816, 8, 22, 11
NEG = -1.0e30
EPS = 1e-6
SLOT = 2048
WSLOT = HC * 128
GRP = 5

PAIR_TILES = [("w_kv", 0, "k"), ("attn_w_q", 0, "q"), ("w_kv", 1, "k"), ("attn_w_q", 1, "q"), ("w_kv", 2, "k"),
              ("attn_w_q", 2, "q"), ("w_kv", 0, "v"), ("w_kv", 1, "v"), ("w_kv", 2, "v")]
HEADS = [(kind, x) for x in range(4) for kind in "sr"]
HEAD_TILES = {"r": (("k", 4), ("q", 0), ("v", 8), ("g", 12)), "s": (("k", 20), ("q", 16), ("v", 24))}



def plan():
    def ada(name, layer, first, blocks):
        return [("ada", first + i, [(name, layer, 0, KC, b, 1) for b in blocks[i:i + 2]])
                for i in range(0, len(blocks), 2)]

    def pairs(tiles):
        return [("main", None, tiles[i:i + 2]) for i in range(0, len(tiles), 2)]

    def mix(main, side, n=1):
        out, side = [], list(side)
        for m in main:
            out.append(m)
            out += side[:n]
            side = side[n:]
        return out, side

    def square(name, layer, blocks):
        return [(name, layer, 0, KC, n, 1) for n in blocks]

    def ffn(gate, up, down, layer):
        out = []
        for half in range(2):
            for j in range(half * HC, half * HC + HC):
                out.append(("main", None, [(gate[0], layer, 0, KC, gate[1] + j, 1),
                                           (up[0], layer, 0, KC, up[1] + j, 1)]))
            out += [("main", None, [(down, layer, half * HC, HC, n, 1)]) for n in range(8)]
        return out

    units = []
    shift, scale = ada("ada_w", 0, 0, list(range(8))), ada("ada_w", 0, 8, list(range(8, 16)))
    for i in range(4):
        units += [shift[i], scale[i], ("main", None, [("pool_w_in", 0, 2 * i, 2, 8 - GRP, GRP)])]
    side = ada("ada_w", 0, 16, list(range(16, 48)))
    pool = pairs(square("pool_w_in", 0, range(8 - GRP)) + square("pool_w_grp", 0, range(2))
                 + square("pool_w_out", 0, range(8)))
    units += pool[:1]
    out, side = mix(pool[1:], side, 2)
    units += out
    side = side + ada("ada_w", 1, 48, list(range(48))) + ada("kv_ada_w", None, 96, list(range(16)))
    out, side = mix(ffn(("ffn_w_up", 0), ("ffn_w_up", FC), "ffn_w_down", 0), side)
    assert not side
    units += out
    qkv = []
    for p in range(8):
        for name, g, what in PAIR_TILES:
            qkv.append((name, 0 if what == "q" else None, 0, KC, (24 if what == "v" else 0) + 8 * g + p, 1))
    units += pairs(qkv)
    units += pairs(square("attn_w_o", 0, range(8)))
    units += ffn(("ffn_w_up", 0), ("ffn_w_up", FC), "ffn_w_down", 1)
    for l in range(2):
        w = []
        for kind, x in HEADS:
            w += square("w_in_2", l, [b + x for _, b in HEAD_TILES[kind]])
        units += pairs(w)
        units += pairs(square("w_out_2", l, range(8)))
        units += ffn(("w_gate_2", 0), ("w_up_2", 0), "w_down_2", l)
    return units


def words(tile):
    return tile[3] * tile[5] * 128


COLS = [("ada_b", 96), ("kv_ada_b", 16), ("norm1_g", 16), ("norm2_g", 16), ("pool_scale", 8),
        ("kv_norm_g", 8), ("final_g", 8), ("norm1_g_2", 16), ("norm2_g_2", 16), ("final_g_2", 8),
        ("ret_norm_g_2", 8), ("sb_norm_g_2", 8), ("ffn_conv_w", 132), ("ffn_conv_b", 44)]
COL = {}
NCOL = 0
for _n, _k in COLS:
    COL[_n] = NCOL
    NCOL += _k


def slopes():
    def pow2(m):
        start = 2.0 ** (-(2.0 ** -(math.log2(m) - 3)))
        return [start ** (i + 1) for i in range(m)]
    s = np.asarray(pow2(32) + pow2(64)[0::2][:16], dtype=np.float32)
    return (-np.sort(-s)).reshape(3, 16)


def tables():
    p = np.arange(128)[:, None]
    q = np.arange(128)[None, :]
    base = np.zeros((128, 704), np.float32)
    base[:, 0:128] = p == q
    base[:, 128:256] = 1.0
    base[:, 256:384] = -(p > q).astype(np.float32)
    base[:, 384:512] = -1.0
    base[:, 512:640] = p < q
    for g, w in enumerate((2, 4, 8, 16)):
        base[:, 640 + 16 * g:656 + 16 * g] = 1.0 / np.minimum(np.arange(16) + 1, w).astype(np.float32)[None, :]
    att = np.zeros((128, 1152), np.float32)
    for n in range(7):
        delta = 4 * (p - q) + (3 - n)
        att[:, 128 * n:128 * n + 128] = np.where((delta >= 0) & (delta <= 128), -delta, NEG)
    att[:, 896:1024] = np.where(p >= q, -4 * (p - q), NEG)
    att[:, 1024:1152] = np.where((p >= q) & ((p - q) % 4 == 0), -4 * (p - q), NEG)
    ret = np.zeros((128, 3072), np.float32)
    t = np.arange(512)[None, :]
    for h in range(4):
        lg = np.log1p(-np.exp2(-5.0 - h))
        w = np.exp(lg * np.abs(t - p)) * 128.0 ** -0.5
        ret[:, 512 * h:512 * h + 512] = np.where(t // 64 >= p // 64, w, 0.0)
    inv = (1.0 / (np.float32(10000.0) ** (np.arange(0, 128, 2, dtype=np.float32) / np.float32(128)))).astype(np.float32)
    ang = (np.arange(512, dtype=np.float32)[None, :] * inv[:, None]).astype(np.float32)
    ret[:, 2048:2560] = np.concatenate([np.cos(ang), np.cos(ang)])
    ret[:, 2560:3072] = np.concatenate([-np.sin(ang), np.sin(ang)])
    return base, att, ret


class Engine:

    def __init__(self, ns, sem):
        self.ns, self.sem, self.n, self.met = ns, sem, 0, {}

    def wait(self, *tokens):
        for t in tokens:
            if t is None:
                continue
            if isinstance(t, list):
                self.wait(*t)
                continue
            sem, value = t
            if self.met.get(id(sem), 0) < value:
                self.ns.wait_ge(sem, value)
                self.met[id(sem)] = value

    def sig(self, ins):
        ins.then_inc(self.sem, 1)
        self.n += 1
        return (self.sem, self.n)

    def last(self):
        return (self.sem, self.n)


class Slot:

    def __init__(self, sem):
        self.sem, self.n = sem, 0

    def sig(self, ins):
        ins.then_inc(self.sem, 16)
        self.n += 16
        return (self.sem, self.n)


def program(nc, stream, cd, colsd, xt, basd, attd, retd, out):
    units = plan()
    usize = [sum(words(t) for t in u[2]) for u in units]
    offs = np.concatenate([[0], np.cumsum([128 * n for n in usize])])
    tiles = [(u, j) for u, unit in enumerate(units) if unit[0] == "main" for j in range(len(unit[2]))]
    SL = slopes()
    top = ExitStack()
    with top:
        def sbuf(name, n, dt=F32, ctx=top):
            return ctx.enter_context(nc.sbuf_tensor(name, [128, n], dt))

        def sem(name):
            return top.enter_context(nc.semaphore(name))

        XT = sbuf("XT", 4096)
        H1H, H1L = sbuf("H1H", 4096, F32R), sbuf("H1L", 4096, F32R)
        RAW = [sbuf(f"RAW{i}", SLOT) for i in range(2)]
        WH = [sbuf(f"WH{i}", WSLOT, F32R) for i in range(3)]
        WL = [sbuf(f"WL{i}", WSLOT, F32R) for i in range(3)]
        SS, SG = sbuf("SS", 512), sbuf("SG", 512)
        CO = sbuf("CO", NCOL)
        MOD = sbuf("MOD", 112)
        AB = sbuf("AB", 40)
        KON = sbuf("KON", 2)
        BAS = sbuf("BAS", 704)
        PS = [top.enter_context(nc.psum_tensor(f"PS{i}", [128, 512], F32)) for i in range(8)]
        free = [None] * 8

        PE, DVE = Engine(nc.tensor, sem("pe")), Engine(nc.vector, sem("dve"))
        SC, PO = Engine(nc.scalar, sem("act")), Engine(nc.gpsimd, sem("pool"))
        SP = Engine(nc.sync, None)
        raw = [Slot(sem(f"raw{i}")) for i in range(2)]
        ara = [Slot(sem(f"ara{i}")) for i in range(3)]
        s_c, s_x, s_co, s_bas, s_att, s_ret = (Slot(sem(n)) for n in ("d_c", "d_x", "d_co", "d_bas", "d_att", "d_ret"))
        s_out = Slot(sem("d_out"))

        IDENT, ONES, UNEG, NONES = (BAS[:, 128 * i:128 * i + 128] for i in range(4))
        STRICT = BAS[:, 512:640]
        ONE, EPSC = KON[:, 0:1], KON[:, 1:2]
        top.enter_context(nc.Block())

        def chunk(buf, k):
            return buf[:, 512 * k:512 * k + 512]

        def xk(k):
            return chunk(XT, k)

        def cols(name, i, n):
            return CO[:, COL[name] + i:COL[name] + i + n]

        def col(name, i):
            return cols(name, i, 1)

        def act(out_, in_, fn=ACT.Copy, w=(), **kw):
            SC.wait(*w)
            return SC.sig(nc.scalar.activation(out_, in_, fn, **kw))

        def tt(out_, a, b, op, w=(), e=None):
            e = e or DVE
            e.wait(*w)
            return e.sig(e.ns.tensor_tensor(out_, a, b, op))

        def stt(out_, a, s, b, op0, op1, w=()):
            DVE.wait(*w)
            return DVE.sig(nc.vector.scalar_tensor_tensor(out_, a, s, b, op0, op1))

        def ts(out_, a, s1, s2, op0, op1=None, w=()):
            DVE.wait(*w)
            if op1 is None:
                return DVE.sig(nc.vector.tensor_scalar(out_, a, s1, None, op0))
            return DVE.sig(nc.vector.tensor_scalar(out_, a, s1, s2, op0, op1))

        def mms(items, w=()):
            PE.wait(*w)
            for it in items:
                if len(it) > 5:
                    PE.wait(it[5])
                ins = nc.tensor.matmul(it[0], it[1], it[2], start=it[3], stop=it[4], skip_group_check=True)
            return PE.sig(ins)

        def turn4(bk, srcs, w):
            PE.wait(*w, free[bk], bastok)
            for n, src in enumerate(srcs):
                ins = nc.tensor.transpose(PS[bk][:, 128 * n:128 * n + 128], src, IDENT)
            return PE.sig(ins)

        def table(name):
            nc.scalar.preload_act_table_set(name + "_and_others")

        nload = [0]
        order = {"main": 0, "ada": 0}
        place, loaded, ready_at = {}, {}, {}
        rawfree, arafree = [None, None], [None] * 3
        nunit, ntile = [0], [0]
        wfree = [None] * 3
        wtok = {}
        usepool = [False]
        ahead = [0]
        AR, condtok, modtok = [], [None], [None]

        def load():
            while nload[0] < len(units):
                u = nload[0]
                kind = units[u][0]
                n = order[kind]
                ring = 2 if kind == "main" else 3
                if n >= ring and not ready_at.get((kind, n - ring)):
                    return
                i = n % ring
                place[u] = i
                SP.wait((rawfree if kind == "main" else arafree)[i])
                src = stream[int(offs[u]):int(offs[u + 1])].rearrange("(p n) -> p n", p=128)
                dst = (RAW if kind == "main" else AR)[i]
                slot = (raw if kind == "main" else ara)[i]
                loaded[u] = slot.sig(nc.sync.dma_start(dst[:, 0:usize[u]], src))
                order[kind] += 1
                nload[0] += 1

        seen = {"main": 0, "ada": 0}

        def finished(kind):
            ready_at[(kind, seen[kind])] = True
            seen[kind] += 1
            load()

        def ada_unit(u):
            i = place[u]
            first = units[u][1]
            for q in range(2):
                src = AR[i][:, 1024 * q:1024 * q + 1024]
                bias = col("ada_b", first + q) if first < 96 else col("kv_ada_b", first - 96 + q)
                DVE.wait(loaded[u], condtok[0], cotok)
                t = DVE.sig(nc.vector.tensor_tensor_reduce(src, src, COND[:, :], 1.0, bias, ALU.mult, ALU.add,
                                                           MOD[:, first + q:first + q + 1]))
            arafree[i] = modtok[0] = t
            finished("ada")

        def prepare(t):
            while ntile[0] <= t and ntile[0] < len(tiles):
                u, j = tiles[ntile[0]]
                while nunit[0] < u:
                    if units[nunit[0]][0] == "ada":
                        ada_unit(nunit[0])
                    nunit[0] += 1
                spec = units[u][2][j]
                base = sum(words(x) for x in units[u][2][:j])
                n, i, s = words(spec), place[u], ntile[0] % 3
                src = RAW[i][:, base:base + n]
                hi = act(WH[s][:, 0:n], src, w=(loaded[u], wfree[s]))
                e = PO if usepool[0] else DVE
                lo = tt(WL[s][:, 0:n], src, WH[s][:, 0:n].bitcast(F32), ALU.subtract, w=(hi, loaded[u], wfree[s]),
                        e=e)
                wtok[ntile[0]] = lo
                if j == len(units[u][2]) - 1:
                    rawfree[i] = lo
                    nunit[0] = u + 1
                    finished("main")
                ntile[0] += 1

        cur = [0]

        def take(name):
            t = cur[0]
            cur[0] += 1
            u, j = tiles[t]
            assert units[u][2][j][0] == name, (name, units[u][2][j])
            prepare(t)
            prepare(t + ahead[0])
            return t % 3, wtok[t], units[u][2][j]

        ring = [0]
        ALLB = (0, 1, 2, 3, 4, 5, 6)

        def bank(banks=ALLB):
            ring[0] += 1
            return banks[ring[0] % len(banks)]

        def three(bank_ap, s, o, hi, lo, first, last, rt=None):
            wh, wl = WH[s][:, o:o + 128], WL[s][:, o:o + 128]
            return [(bank_ap, wh, hi, first, False, rt), (bank_ap, wh, lo, False, False),
                    (bank_ap, wl, hi, False, last)]

        early_tiles = []

        def tile(name, hl, ready=None, banks=ALLB):
            if early_tiles:
                t, bk, m = early_tiles.pop(0)
                prepare(t + ahead[0])
                return bk, m
            s, tok, spec = take(name)
            bk = bank(banks)
            hi, lo = hl
            items = []
            for k in range(spec[3]):
                items += three(PS[bk][:, :], s, 128 * k, chunk(hi, k), chunk(lo, k), k == 0, k == spec[3] - 1,
                               ready[k] if ready else None)
            m = mms(items, w=(tok, free[bk]))
            wfree[s] = m
            return bk, m

        def group(names, hls, readys, korder=tuple(range(8)), split=4, hooks=(), banks=ALLB):
            t0 = cur[0]
            hooks = dict(hooks)
            prepare(t0 + len(names) - 1)
            got = []
            for n in names:
                t = cur[0]
                cur[0] += 1
                u, j = tiles[t]
                assert units[u][2][j][0] == n
                got.append((t, bank(banks)))
            toks = []

            def part(x, ks):
                t, bk = got[x]
                items = []
                for k in ks:
                    items += three(PS[bk][:, :], t % 3, 128 * k, chunk(hls[x][0], k), chunk(hls[x][1], k),
                                   k == korder[0], k == korder[-1], readys[x][k] if readys[x] else None)
                return mms(items, w=(wtok[t], free[bk]))

            for n, k in enumerate(korder[:split]):
                for x in range(len(names)):
                    part(x, [k])
                if n in hooks:
                    hooks[n]()
            for x in range(len(names)):
                m = part(x, korder[split:])
                wfree[got[x][0] % 3] = m
                early_tiles.append((got[x][0], got[x][1], m))

        def barrier(*others):
            toks = [e.last() for e in (PE, DVE, SC, PO) if e.n]
            for e in (DVE, SC, PO, *others):
                e.wait(*toks)

        ssa, sga = [None], [None]
        sq7 = [None]

        def norm_bufs(ctx, tag):
            names = ["SQ0", "SQ1", "R", "T0", "T1", "T2", "V0", "V1", "V2"]
            b = {n: sbuf(n + tag, 512, F32, ctx) for n in names}
            b.update(SQ=[b["SQ0"], b["SQ1"]], T=[b["T0"], b["T1"], b["T2"]], V=[b["V0"], b["V1"], b["V2"]],
                     sq=[None, None], tf=[None] * 3, vf=[None] * 3, n=0)
            return b

        def add_square(b, k, w, acc=None, state=None, scale=1.0):
            acc, state = acc or SS, state or ssa
            if k == 0:
                state[0] = act(acc[:, :], xk(0), ACT.Square, scale=scale, w=(w, state[0]))
                return
            i = b["n"] % 2 if k < 7 or acc is SG else 1
            b["n"] = i + 1
            t = act(b["SQ"][i][:, :], xk(k), ACT.Square, scale=scale, w=(w, b["sq"][i]))
            if k == 7 and acc is SS:
                sq7[0] = b["sq"][1] = t
                return
            state[0] = b["sq"][i] = tt(acc[:, :], acc[:, :], b["SQ"][i][:, :], ALU.add, w=(t, state[0]))

        def rsqrt_of(bk, out_, scale, w):
            t = free[bk] = act(out_, PS[bk][:, :], ACT.Ln, bias=EPSC, scale=scale, w=(*w, kontok))
            return act(out_, out_, ACT.Exp, scale=-0.5, w=(t,))

        def norm_r(b):
            i = bank()
            mms([(PS[i][:, :], ONES, SS[:, :], True, False)], w=(ssa[0], free[i], bastok))
            m = mms([(PS[i][:, :], ONES, b["SQ"][1][:, :], False, True)], w=(sq7[0],))
            ssa[0] = b["sq"][1] = m
            return rsqrt_of(i, b["R"][:, :], 1.0 / D, (m,))

        def norm_k(b, r, k, outs, w=()):
            i = k % 3
            toks = []
            if outs[0][3] is None:
                hi, lo, gain, _, view = outs[0]
                t = stt(b["T"][i][:, :], xk(k), gain[:, k:k + 1], b["R"][:, :], ALU.mult, ALU.mult,
                        w=(r, *w, b["tf"][i]))
                h = act(view(chunk(hi, k)), b["T"][i][:, :], w=(t,))
                l = tt(view(chunk(lo, k)), b["T"][i][:, :], view(chunk(hi, k)).bitcast(F32), ALU.subtract,
                       w=(t, h), e=PO if k % 2 else DVE)
                b["tf"][i] = l
                return [l]
            t = tt(b["T"][i][:, :], xk(k), b["R"][:, :], ALU.mult, w=(r, *w, b["tf"][i]))
            used = []
            for n, (hi, lo, gain, shift, view) in enumerate(outs):
                j = (k * len(outs) + n) % 3
                v = b["V"][j]
                if n == 0:
                    t2 = act(v[:, :], b["T"][i][:, :], ACT.Identity, scale=gain[:, k:k + 1], bias=shift[:, k:k + 1],
                             w=(t, b["vf"][j], *w))
                else:
                    t2 = ts(v[:, :], b["T"][i][:, :], gain[:, k:k + 1], shift[:, k:k + 1], ALU.mult, ALU.add,
                            w=(t, b["vf"][j]))
                h = act(view(chunk(hi, k)), v[:, :], w=(t2,))
                pool = (n == 0) if len(outs) > 1 else (k % 2 == 1)
                l = tt(view(chunk(lo, k)), v[:, :], view(chunk(hi, k)).bitcast(F32), ALU.subtract, w=(t2, h),
                       e=PO if pool else DVE)
                b["vf"][j] = l
                toks.append(l)
                used.append(t2)
            b["tf"][i] = used
            return toks

        def norm_apply(b, r, outs, w=()):
            got = [norm_k(b, r, k, outs, w) for k in range(8)]
            return [[g[n] for g in got] for n in range(len(outs))]

        def plain(ap):
            return ap

        def permuted(ap):
            return ap.rearrange("p (r j) -> p j r", r=4)

        def mod(first, n=8):
            return MOD[:, first:first + n]

        def gains(at, name, i, scale_col, n=8):
            return stt(AB[:, at:at + n], mod(scale_col, n), 1.0, cols(name, i, n), ALU.add, ALU.mult,
                       w=(modtok[0], cotok))

        def residual(n, b, m, bk, gcol=None, square=True, second=False):
            if gcol is None:
                t = tt(xk(n), PS[bk][:, :], xk(n), ALU.add, w=(m,))
            else:
                t = stt(xk(n), PS[bk][:, :], gcol, xk(n), ALU.mult, ALU.add, w=(m,))
            free[bk] = t
            if square:
                add_square(b, n, t)
                if second:
                    add_square(b, n, t, SG, sga, col("final_g", n))
            return t

        def split_out(bk, hi, lo, m, scale, w=()):
            h = act(hi, PS[bk][:, :], scale=scale, w=(m, *w))
            l = stt(lo, PS[bk][:, :], scale, hi.bitcast(F32), ALU.mult, ALU.subtract, w=(h,))
            free[bk] = l
            return l

        H1 = (H1H, H1L)

        early = ExitStack()
        AR += [sbuf(f"AR{i}", SLOT, F32, early) for i in range(3)]
        COND = sbuf("COND", 1024, F32, early)
        nb = norm_bufs(early, "a")
        table("silu")
        ctok = s_c.sig(nc.scalar.dma_start(COND[:, :], cd.partition_broadcast(128)))
        cotok = s_co.sig(nc.sync.dma_start(CO[:, :], colsd))
        xtok = s_x.sig(nc.sync.dma_start(XT[:, :].rearrange("p (k t) -> p k t", k=8),
                                         xt.rearrange("(k p) t -> p k t", p=128)))
        bastok = s_bas.sig(nc.sync.dma_start(BAS[:, :], basd))
        load()
        PO.sig(nc.gpsimd.memset(ONE, 1.0))
        kontok = PO.sig(nc.gpsimd.memset(EPSC, EPS))
        condtok[0] = act(COND[:, :], COND[:, :], ACT.Silu, w=(ctok,))
        table("natural_log_exp")
        for k in range(8):
            add_square(nb, k, xtok)
        r = norm_r(nb)
        usepool[0] = True
        h1 = []
        kb = [0, 1, 2, 3, 4]
        for i in range(4):
            s, tok, spec = take("pool_w_in")
            ta = gains(2 * i, "norm1_g", 2 * i, 8 + 2 * i, 2)
            for k in (2 * i, 2 * i + 1):
                h1 += norm_k(nb, r, k, [(H1H, H1L, AB[:, 0:8], mod(0), plain)], w=(ta,))
            for j in range(2):
                for x in range(GRP):
                    k = 2 * i + j
                    m = mms(three(PS[kb[x]][:, :], s, 128 * (GRP * j + x), chunk(H1H, k), chunk(H1L, k),
                                  k == 0, k == 7, h1[k]), w=(tok, free[kb[x]]))
            wfree[s] = m
        ahead[0] = 2

        pool = ExitStack()
        H2H, H2L = sbuf("H2Ha", 4096, F32R, pool), sbuf("H2La", 4096, F32R, pool)
        U = [sbuf(f"U{i}", 528, F32, pool) for i in range(2)]
        V = [[sbuf(f"V{i}{j}", 528, F32, pool) for i in range(2)] for j in range(2)]
        tz = None
        for t_ in (*U, *V[0], *V[1]):
            tz = DVE.sig(nc.vector.memset(t_[:, 0:16], 0.0))
        ufree, vfree, h2 = [None, None], [None, None], [None] * 8

        def pooled(n, bk, m):
            g, i = n // 2, n % 2
            e = PO if i else DVE
            u = U[i]
            t = free[bk] = act(u[:, 16:528], PS[bk][:, :], w=(m, ufree[i], tz))
            src, sh, dst = u, 1, 0
            e.wait(vfree[i])
            for _ in range(g + 1):
                d = V[i][dst]
                t = tt(d[:, 16:528], src[:, 16:528], src[:, 16 - sh:528 - sh], ALU.add, w=(t, tz), e=e)
                src, sh, dst = d, sh * 2, 1 - dst
            p = V[i][dst]
            t1 = stt(p[:, 16:528], src[:, 16:528], 1.0 / sh, u[:, 16:528], ALU.mult, ALU.subtract, w=(t,))
            t2 = tt(p[:, 16:16 + sh], src[:, 16:16 + sh], BAS[:, 640 + 16 * g:640 + 16 * g + sh], ALU.mult,
                    w=(t1, bastok))
            t3 = tt(p[:, 16:16 + sh], p[:, 16:16 + sh], u[:, 16:16 + sh], ALU.subtract, w=(t2,))
            ufree[i] = t3
            hh = act(chunk(H2H, n), p[:, 16:528], w=(t3,))
            h2[n] = vfree[i] = tt(chunk(H2L, n), p[:, 16:528], chunk(H2H, n).bitcast(F32), ALU.subtract,
                                  w=(t3, hh), e=e)

        for x in range(GRP):
            pooled(8 - GRP + x, kb[x], m)
        for n in range(8 - GRP):
            bk, m = tile("pool_w_in", H1, h1, banks=(5, 6))
            pooled(n, bk, m)
        gfree = PE.last()
        h1 = [None] * 8
        for d in range(2):
            s, tok, _ = take("pool_w_grp")
            for g in range(4):
                bk = bank()
                items = []
                for i in range(2):
                    c = 2 * g + i
                    items += three(PS[bk][:, :], s, 128 * c, chunk(H2H, c), chunk(H2L, c), i == 0, i == 1, h2[c])
                m = mms(items, w=(tok, free[bk]))
                n = 2 * g + d
                h1[n] = split_out(bk, chunk(H1H, n), chunk(H1L, n), m, col("pool_scale", n), w=(gfree,))
            wfree[s] = m
        for n in range(8):
            bk, m = tile("pool_w_out", H1, h1)
            residual(n, nb, m, bk, MOD[:, 16 + n:17 + n])
        pool.close()
        barrier()

        def ffn(tag, b, ctx, names, h, conv, gate, second=False):
            GH, GL = sbuf(f"GH{tag}", HC * 512, F32R, ctx), sbuf(f"GL{tag}", HC * 512, F32R, ctx)
            Y = [sbuf(f"Y{tag}{i}", 512, F32, ctx) for i in range(2)]
            SI = [sbuf(f"SI{tag}{i}", 512, F32, ctx) for i in range(2)]
            gfree = None
            gt = [None, None]
            na, nv, nd = names
            group([na, nv, na], [H1] * 3, [h] * 3)
            for half in range(2):
                ready = []
                for jj in range(HC):
                    j, i = half * HC + jj, jj % 2
                    ba, ma = tile(na, H1)
                    if conv is not None:
                        cw = [col("ffn_conv_w", conv * 66 + q * 22 + j) for q in range(3)]
                        y = act(Y[i][:, :], PS[ba][:, :], ACT.Identity, scale=cw[2],
                                bias=col("ffn_conv_b", conv * 22 + j), w=(ma, gt[i]))
                        y = stt(Y[i][:, 1:512], PS[ba][:, 0:511], cw[1], Y[i][:, 1:512], ALU.mult, ALU.add, w=(y,))
                        y = stt(Y[i][:, 2:512], PS[ba][:, 0:510], cw[0], Y[i][:, 2:512], ALU.mult, ALU.add, w=(y,))
                        free[ba] = y
                        si = act(SI[i][:, :], Y[i][:, :], ACT.Silu, w=(y,))
                    else:
                        si = free[ba] = act(SI[i][:, :], PS[ba][:, :], ACT.Silu, w=(ma, gt[i]))
                    bv, mv = tile(nv, H1)
                    g = free[bv] = tt(SI[i][:, :], SI[i][:, :], PS[bv][:, :], ALU.mult, w=(mv, si))
                    g1 = act(chunk(GH, jj), SI[i][:, :], w=(g, gfree))
                    g2 = tt(chunk(GL, jj), SI[i][:, :], chunk(GH, jj).bitcast(F32), ALU.subtract, w=(g1,))
                    gt[i] = g2
                    ready.append(g2)
                if half:
                    table("natural_log_exp")
                for n in range(8):
                    bk, m = tile(nd, (GH, GL), ready)
                    gfree = m
                    residual(n, b, m, bk, None if gate is None else MOD[:, gate + n:gate + n + 1],
                             square=half == 1, second=second)

        prepare(cur[0] + 2)
        ta = gains(8, "norm2_g", 0, 32)
        r = norm_r(nb)
        table("silu")
        (h,) = norm_apply(nb, r, [(H1H, H1L, AB[:, 8:16], mod(24), plain)], w=(ta, PE.last()))
        ffn("a", nb, early, ("ffn_w_up", "ffn_w_up", "ffn_w_down"), h, 0, 40)
        usepool[0] = False
        prepare(cur[0] + 2)
        ta1 = gains(16, "norm1_g", 8, 48 + 8)
        takv = gains(24, "kv_norm_g", 0, 96 + 8)
        gains(32, "norm2_g", 8, 48 + 32)
        r = norm_r(nb)
        rsave = act(SG[:, :], nb["R"][:, :], w=(r,))
        early.close()
        barrier()

        att = ExitStack()
        H2H, H2L = sbuf("H2Hb", 4096, F32R, att), sbuf("H2Lb", 4096, F32R, att)
        H2 = (H2H, H2L)
        ATT = sbuf("ATT", 1152, F32, att)
        QT = [sbuf(f"QT{i}", 1536, F32, att) for i in range(2)]
        KT = [sbuf(f"KT{i}", 1536, F32, att) for i in range(2)]
        VV = [sbuf(f"VV{i}", 1536, F32, att) for i in range(2)]
        OT = sbuf("OT", 4096, F32, att)
        VF = sbuf("VF", 512, F32, att)
        STAT = sbuf("STAT", 16, F32, att)
        sub = ExitStack()
        nb = norm_bufs(sub, "b")
        nb["R"] = SG
        hq, hkv = norm_apply(nb, rsave, [(H1H, H1L, AB[:, 16:24], mod(48), permuted),
                                         (H2H, H2L, AB[:, 24:32], mod(96), permuted)], w=(ta1, takv, PE.last()))
        SP.wait(PE.last(), DVE.last(), SC.last(), PO.last())
        atok = s_att.sig(nc.sync.dma_start(ATT[:, :], attd))
        subtok = [DVE.last(), SC.last(), PO.last()]
        sub.close()
        SB = [sbuf(f"SB{i}", 1536, F32, att) for i in range(2)]
        PT = [sbuf(f"PT{i}", 1536, F32, att) for i in range(2)]

        used, vtok, defer = {}, [None], []
        qkvtok = {}
        group(["w_kv", "attn_w_q", "w_kv"], [H2, H1, H2], [hkv, hq, hkv], banks=(0, 1, 2))

        def project(t):
            p, x = t // 9, t % 9
            i = p % 2
            name, g, what = PAIR_TILES[x]
            bk, m = tile(name, H1 if what == "q" else H2, banks=(0, 1))
            while defer:
                defer.pop(0)()
            if what == "v":
                tv = free[bk] = act(VF[:, :], PS[bk][:, :], w=(m, vtok[0]))

                def rest():
                    m2 = vtok[0] = turn4(5, [VF[:, 128 * q:128 * q + 128] for q in range(4)], (tv,))
                    qkvtok[p] = free[5] = act(chunk(VV[i], g), PS[5][:, :], w=(m2, used.get(p - 2)))
                defer.append(rest)
            else:
                dst = (QT if what == "q" else KT)[i]
                qkvtok[p] = free[bk] = act(chunk(dst, g), PS[bk][:, :], scale=0.125 if what == "q" else 1.0,
                                           w=(m, used.get(p - 2)))

        sbfree, ptfree = [subtok, subtok], [subtok, subtok]
        stok, ttok, otok = {}, {}, {}

        def scores(p, r_):
            i, n = p % 2, (4 * p + r_) % 2
            sb = SB[n]
            tok = []
            for hh in range(2):
                head = 2 * p + hh
                po = slice(64 * hh, 64 * hh + 64)
                q = [QT[i][po, 512 * g + 128 * r_:512 * g + 128 * r_ + 128] for g in range(3)]
                m0 = mms([(PS[2 + hh][:, :], q[0], KT[i][po, 0:512], True, True)], w=(free[2 + hh], qkvtok[p]))
                m1 = mms([(PS[4][:, 256 * hh + 128 * g - 128:256 * hh + 128 * g], q[g],
                           KT[i][po, 512 * g + 128 * r_:512 * g + 128 * r_ + 128], hh == 0 and g == 1, True)
                          for g in (1, 2)], w=(free[4],) if hh == 0 else (tok[0][1],))
                tok.append((m0, m1))
            for hh in range(2):
                head = 2 * p + hh
                m0, m1 = tok[hh]
                o = 768 * hh
                free[2 + hh] = stt(sb[:, o:o + 512], ATT[:, 128 * (3 - r_):128 * (3 - r_) + 512],
                                   float(SL[0][head]), PS[2 + hh][:, :], ALU.mult, ALU.add,
                                   w=(m0, sbfree[n], atok))
                DVE.wait(tok[1][1])
                for g in (1, 2):
                    t1 = stt(sb[:, o + 384 + 128 * g:o + 512 + 128 * g], ATT[:, 768 + 128 * g:896 + 128 * g],
                             float(SL[g][head]), PS[4][:, 256 * hh + 128 * g - 128:256 * hh + 128 * g],
                             ALU.mult, ALU.add)
                z = 8 * n + 4 * hh
                DVE.wait(t1)
                t2 = DVE.sig(nc.vector.tensor_reduce(STAT[:, z:z + 1], sb[:, o:o + 768], AX_X, ALU.max))
                t3 = ts(STAT[:, z + 1:z + 2], STAT[:, z:z + 1], -1.0, None, ALU.mult, w=(t2,))
                stok[(p, r_, hh)] = act(sb[:, o:o + 768], sb[:, o:o + 768], ACT.Exp, bias=STAT[:, z + 1:z + 2],
                                        scale=1.0, accum_out=STAT[:, z + 2:z + 3], w=(t3,))
            free[4] = t1

        def norms(p, r_):
            n = (4 * p + r_) % 2
            for hh in range(2):
                z, o = 8 * n + 4 * hh, 768 * hh
                DVE.wait(stok[(p, r_, hh)])
                t = DVE.sig(nc.vector.reciprocal(STAT[:, z + 3:z + 4], STAT[:, z + 2:z + 3]))
                stok[(p, r_, hh)] = ts(SB[n][:, o:o + 768], SB[n][:, o:o + 768], STAT[:, z + 3:z + 4], None,
                                       ALU.mult, w=(t,))

        def transposes(p, r_):
            n = (4 * p + r_) % 2
            sb, pt = SB[n], PT[n]
            w = (stok[(p, r_, 0)], stok[(p, r_, 1)])
            got = []
            for c in range(3):
                bk = 6 + (3 * (4 * p + r_) + c) % 2 if p < 7 else 7
                m = turn4(bk, [sb[:, 512 * c + 128 * q:512 * c + 128 * q + 128] for q in range(4)], w)
                if c == 1:
                    DVE.wait(m, ptfree[n])
                    t = DVE.sig(nc.vector.tensor_copy(chunk(pt, c), PS[bk][:, :]))
                else:
                    t = act(chunk(pt, c), PS[bk][:, :], w=(m, ptfree[n]))
                free[bk] = t
                got.append(t)
            sbfree[n] = m
            ttok[(p, r_)] = got

        def values(p, r_):
            i, n = p % 2, (4 * p + r_) % 2
            pt = PT[n]
            PE.wait(ttok[(p, r_)], free[5])
            for c in range(6):
                g, kt = (0, c) if c < 4 else (c - 3, r_)
                for hh in range(2):
                    v = VV[i][:, 512 * g + 128 * kt + 64 * hh:512 * g + 128 * kt + 64 * hh + 64]
                    ins = nc.tensor.matmul(PS[5][64 * hh:64 * hh + 64, 0:128], v,
                                           pt[:, 768 * hh + 128 * c:768 * hh + 128 * c + 128],
                                           start=c == 0, stop=c == 5, skip_group_check=True)
            m = ptfree[n] = PE.sig(ins)
            if r_ == 3:
                used[p] = m
            free[5] = otok[p] = act(OT[:, 512 * p + 128 * r_:512 * p + 128 * r_ + 128], PS[5][:, 0:128], w=(m,))

        events = []
        for g in range(32):
            at = 9 * (g // 4 + 1) + 2.25 * (g % 4)
            events += [(at + 0.6, g, scores), (at + 2.2, g, norms), (at + 3.3, g, transposes), (at + 4.9, g, values)]
        events.sort(key=lambda e: (e[0], e[1]))

        def run_events(until):
            while events and events[0][0] <= until:
                _, g, fn = events.pop(0)
                fn(g // 4, g % 4)

        for t in range(72):
            run_events(t)
            project(t)
        while defer:
            defer.pop(0)()
        hfree = PE.last()
        oready = [None] * 8

        def natural(ap):
            return ap.rearrange("p (j r) -> p j r", r=4)

        def out_split(k, e):
            src = chunk(OT, k).rearrange("p (r j) -> p j r", r=4)
            t = act(natural(chunk(H1H, k)), src, w=(otok[k], hfree))
            oready[k] = tt(natural(chunk(H1L, k)), src, natural(chunk(H1H, k).bitcast(F32)), ALU.subtract,
                           w=(t, otok[k], hfree), e=e)

        run_events(74.7)
        for k in range(7):
            out_split(k, PO if k % 2 else DVE)
        hooks = {}
        for n in range(7):
            hooks[n] = (lambda n=n: run_events(75.6 + n * 1.5 if n < 6 else 1000))

        def last_hook():
            run_events(1000)
            out_split(7, DVE)
        hooks[6] = last_hook
        group(["attn_w_o"] * 3, [H1] * 3, [oready] * 3, split=7, hooks=hooks.items(), banks=(0, 1, 6))
        barrier()
        att.close()

        lay = ExitStack()
        nb = norm_bufs(lay, "c")
        for n in range(8):
            bk, m = tile("attn_w_o", H1, oready)
            residual(n, nb, m, bk, MOD[:, 64 + n:65 + n])
        prepare(cur[0] + 2)
        r = norm_r(nb)
        table("silu")
        (h,) = norm_apply(nb, r, [(H1H, H1L, AB[:, 32:40], mod(48 + 24), plain)], w=(PE.last(),))
        ffn("b", nb, lay, ("ffn_w_up", "ffn_w_up", "ffn_w_down"), h, 1, 48 + 40, second=True)
        prepare(cur[0] + 2)
        r = norm_r(nb)
        i = bank()
        m = mms([(PS[i][:, :], ONES, SG[:, :], True, True)], w=(sga[0], free[i]))
        T0, T1 = nb["T"][0], nb["T"][1]
        t = tt(T0[:, :], nb["R"][:, :], PS[i][:, :], ALU.mult, w=(r, m))
        t = free[i] = tt(T0[:, :], T0[:, :], nb["R"][:, :], ALU.mult, w=(t,))
        t = act(T0[:, :], T0[:, :], ACT.Ln, bias=EPSC, scale=1.0 / D, w=(t,))
        rtok2 = act(SG[:, :], T0[:, :], ACT.Exp, scale=-0.5, w=(t,))
        xt_ = []
        for k in range(8):
            xt_.append(stt(xk(k), xk(k), col("final_g", k), nb["R"][:, :], ALU.mult, ALU.mult, w=(r,)))
        barrier()
        lay.close()

        for l in range(2):
            lay = ExitStack()
            H2H, H2L = sbuf(f"H2Hc{l}", 4096, F32R, lay), sbuf(f"H2Lc{l}", 4096, F32R, lay)
            H2 = (H2H, H2L)
            nb = norm_bufs(lay, f"d{l}")
            if l == 0:
                nb["R"] = SG
                r = rtok2
            else:
                r = rkeep
                nb["R"] = SG
            (hx,) = norm_apply(nb, r, [(H1H, H1L, cols("norm1_g_2", 8 * l, 8), None, plain)], w=(PE.last(),))
            group(["w_in_2"] * 3, [H1] * 3, [hx] * 3, banks=(0, 1, 2))
            RT = sbuf(f"RT{l}", 3072, F32, lay)
            DEC = [RT[:, 512 * i:512 * i + 512] for i in range(4)]
            COS, SIN = RT[:, 2048:2560], RT[:, 2560:3072]
            Q = [sbuf(f"Q{l}{i}", 512, F32, lay) for i in range(3)]
            K = [sbuf(f"K{l}{i}", 512, F32, lay) for i in range(3)]
            G = [sbuf(f"G{l}{i}", 512, F32, lay) for i in range(2)]
            W = [sbuf(f"W{l}{i}", 512, F32, lay) for i in range(3)]
            VR = sbuf(f"VR{l}", 512, F32, lay)
            TMP = [sbuf(f"TMP{l}{i}", 512, F32, lay) for i in range(2)]
            AA = sbuf(f"AA{l}", 1280, F32, lay)
            SPL = sbuf(f"SPL{l}", 1280, F32, lay)
            OBS = [sbuf(f"OB{l}{i}", 512, F32, lay) for i in range(2)]
            OCS = [sbuf(f"OC{l}{i}", 512, F32, lay) for i in range(2)]
            SP.wait(PE.last(), DVE.last(), SC.last(), PO.last())
            rtok = s_ret.sig(nc.sync.dma_start(RT[:, :], retd))
            tok = {}
            tmpfree = {"k": None, "q": None}
            OFF = [0, 512, 896, 1152]
            WID = [512, 384, 256, 128]
            SBK = [(2, 0), (3, 0), (4, 0), (3, 384)]
            LBK = [(5, 0), (6, 0), (7, 0), (6, 384)]
            mixed = [None] * 8
            defer = []
            jobs = [(n, what) for n in range(8) for what, _ in HEAD_TILES[HEADS[n][0]]]

            def proj(t_):
                n, what = jobs[t_]
                kind, x = HEADS[n]
                i = n % 3
                done = tok.get(("used", n - 3))
                bk, m = tile("w_in_2", H1, banks=(0, 1))
                while defer:
                    defer.pop(0)()
                if what in "kq" and kind == "r":
                    dst = (K if what == "k" else Q)[i]
                    tp = TMP[0 if what == "k" else 1]
                    s1 = act(tp[0:64, :], PS[bk][64:128, :], w=(m, tmpfree[what]))
                    s2 = act(tp[64:128, :], PS[bk][0:64, :])
                    c1 = free[bk] = tt(dst[:, :], PS[bk][:, :], COS, ALU.mult, w=(s2, done, rtok))
                    c2 = tt(tp[:, :], tp[:, :], SIN, ALU.mult, w=(s1, s2, rtok), e=PO)
                    t = tmpfree[what] = tt(dst[:, :], dst[:, :], tp[:, :], ALU.add, w=(c1, c2), e=PO)
                elif what in "kq":
                    dst = (K if what == "k" else Q)[i]
                    t = free[bk] = act(dst[:, :], PS[bk][:, :], scale=1.0 if what == "k" else 128.0 ** -0.5,
                                       w=(m, done))
                elif what == "g":
                    t = free[bk] = act(G[x % 2][:, :], PS[bk][:, :], w=(m, tok.get(("gfree", x % 2))))
                    tok[("g", n)] = t
                else:
                    tv = free[bk] = act(VR[:, :], PS[bk][:, :], w=(m, tok.get("vr")))

                    def rest():
                        m2 = tok["vr"] = turn4(7, [VR[:, 128 * q:128 * q + 128] for q in range(4)], (tv,))
                        tok[("v", n)] = free[7] = act(W[i][:, :], PS[7][:, :], w=(m2, done))
                    defer.append(rest)
                    t = None
                tok.setdefault(n, []).append(t)

            def products(n):
                i = n % 3
                for x in range(4):
                    b_, c0 = SBK[x]
                    m = mms([(PS[b_][:, c0:c0 + WID[x]], K[i][:, 128 * x:128 * x + 128],
                              Q[i][:, 128 * x:512], c0 == 0, True)], w=(free[b_], tok[n]))
                    tok[("z", x)] = m
                return m

            def weighted(n, ready, bk):
                i = n % 3
                its = [(PS[bk][:, 128 * x:512], W[i][:, 128 * x:128 * x + 128], AA[:, OFF[x]:OFF[x] + WID[x]],
                        x == 0, x == 3, ready[x]) for x in range(4)]
                m = mms(its, w=(free[bk], tok[("v", n)]))
                tok["aa"] = tok[("used", n)] = m
                return m

            def r1(n):
                products(n)
                ready = []
                for y in range(4):
                    b_, c0 = SBK[y]
                    t = tt(AA[:, OFF[y]:OFF[y] + WID[y]], PS[b_][:, c0:c0 + WID[y]],
                           DEC[HEADS[n][1]][:, 0:WID[y]], ALU.mult, w=(tok[("z", 3)], rtok, tok.get("aa")))
                    free[b_] = t
                    ready.append(t)
                tok[("rd", n)] = ready

            def r2(n):
                m = weighted(n, tok[("rd", n)], 5)
                tok[("o", n)] = free[5] = act(OBS[1][:, :], PS[5][:, :], w=(m, tok.get("ob1")))

            def r3(n):
                OB, OC = OBS[1], OCS[1]
                m = mms([(PS[6][:, :], ONES, OB[:, :], True, True)], w=(tok[("o", n)], free[6]))
                t = free[6] = stt(OB[:, :], PS[6][:, :], -1.0 / 128, OB[:, :], ALU.mult, ALU.add,
                                  w=(m, tok[("o", n)]))
                tok[("q", n)] = act(OC[:, :], OB[:, :], ACT.Square, w=(t, tok.get("oc1")))

            def s1(n):
                products(n)
                parts, ts_ = [], []
                for y in range(4):
                    b_, c0 = SBK[y]
                    a_ = AA[:, OFF[y]:OFF[y] + WID[y]]
                    ts_.append(act(a_, PS[b_][:, c0:c0 + WID[y]], ACT.Abs, w=(tok[("z", 3)], tok.get("aa"))))
                zt = ts_[3]
                for y in range(4):
                    b_, c0 = SBK[y]
                    z = PS[b_][:, c0:c0 + WID[y]]
                    a_ = AA[:, OFF[y]:OFF[y] + WID[y]]
                    s_ = SPL[:, OFF[y]:OFF[y] + WID[y]]
                    t = act(a_, a_, ACT.Exp, scale=-1.0, w=(ts_[y],))
                    t = act(a_, a_, ACT.Ln, bias=ONE, w=(t, kontok))
                    t = stt(s_, z, 0.0, a_, ALU.max, ALU.add, w=(t, zt, tok.get("sp")))
                    t = free[b_] = tt(a_, z, s_, ALU.subtract, w=(t,))
                    t = tt(s_[:, 0:128], s_[:, 0:128], STRICT, ALU.mult, w=(t,))
                    parts.append(t)
                tok[("parts", n)] = parts

            def s2(n):
                parts = tok[("parts", n)]
                ready = []
                ms = []
                for y in (3, 2, 1, 0):
                    b_, c0 = LBK[y]
                    its = []
                    for j in range(y, 4):
                        its.append((PS[b_][:, c0 + 128 * (j - y):c0 + WID[y]], UNEG if j == y else NONES,
                                    SPL[:, OFF[j]:OFF[j] + WID[j]], j == y and y != 1, j == 3, parts[j]))
                    ms.append(mms(its, w=(free[b_],)))
                tok["sp"] = ms[3]
                ms = ms[::-1]
                for y in (3, 2, 1, 0):
                    b_, c0 = LBK[y]
                    a_ = AA[:, OFF[y]:OFF[y] + WID[y]]
                    t = free[b_] = tt(a_, a_, PS[b_][:, c0:c0 + WID[y]], ALU.add,
                                      w=(ms[1] if y == 3 else ms[y], parts[y]))
                    t = act(a_, a_, ACT.Exp, w=(t,))
                    ready.append(tt(a_[:, 0:128], a_[:, 0:128], STRICT, ALU.mult, w=(t,)))
                tok[("rd", n)] = ready[::-1]

            def s3(n):
                m = weighted(n, tok[("rd", n)], 2)
                tok[("o", n)] = t = free[2] = act(OBS[0][:, :], PS[2][:, :], w=(m, tok.get("ob0")))
                tok[("q", n)] = act(OCS[0][:, :], OBS[0][:, :], ACT.Square, w=(t, tok.get("oc0")))

            def finish(n):
                kind, x = HEADS[n]
                k = x if kind == "r" else 4 + x
                i = 1 if kind == "r" else 0
                OB, OC, bk = OBS[i], OCS[i], 6 if kind == "r" else 7
                m = mms([(PS[bk][:, :], ONES, OC[:, :], True, True)], w=(tok[("q", n)], free[bk]))
                q1 = free[bk] = act(OC[:, :], PS[bk][:, :], ACT.Ln, bias=EPSC, scale=1.0 / 128, w=(m,))
                q2 = act(OC[:, :], OC[:, :], ACT.Exp, scale=-0.5, w=(q1,))
                gc = col("ret_norm_g_2" if kind == "r" else "sb_norm_g_2", 4 * l + x)
                y1 = stt(OB[:, :], OB[:, :], gc, OC[:, :], ALU.mult, ALU.mult, w=(q2, tok[("o", n)], tok[("q", n)]))
                tok[f"oc{i}"] = y1
                if kind == "r":
                    y1 = tt(OB[:, :], OB[:, :], G[x % 2][:, :], ALU.mult, w=(y1, tok[("gs", n)]))
                    tok[("gfree", x % 2)] = y1
                y2 = act(chunk(H2H, k), OB[:, :], w=(y1,))
                y3 = tt(chunk(H2L, k), OB[:, :], chunk(H2H, k).bitcast(F32), ALU.subtract, w=(y2,))
                tok[f"ob{i}"] = mixed[k] = y3

            def gate_silu(n):
                table("silu")
                g = G[HEADS[n][1] % 2]
                tok[("gs", n)] = act(g[:, :], g[:, :], ACT.Silu, w=(tok[("g", n)],))
                table("natural_log_exp")

            events = []
            for x in range(4):
                a, b = 7 * x + 3, 7 * x + 7
                events += [(a + 0.5, 2 * x, s1), (a + 2.5, 2 * x, s2), (a + 3.8, 2 * x, s3), (a + 5, 2 * x, finish),
                           (b + 0.5, 2 * x + 1, r1), (b + 0.6, 2 * x + 1, gate_silu), (b + 1.5, 2 * x + 1, r2),
                           (b + 2.3, 2 * x + 1, r3), (b + 3.2, 2 * x + 1, finish)]
            events.sort(key=lambda e: (e[0], e[1]))

            def run_ev(until, events=events):
                while events and events[0][0] <= until:
                    _, n, fn = events.pop(0)
                    fn(n)

            for t_ in range(28):
                run_ev(t_)
                proj(t_)
            while defer:
                defer.pop(0)()
            run_ev(28.6)
            order_ = (4, 0, 5, 1, 6, 2, 7, 3)
            hooks = {1: lambda: run_ev(29.9), 3: lambda: run_ev(30.5), 5: lambda: run_ev(1000)}
            group(["w_out_2"] * 3, [H2] * 3, [mixed] * 3, korder=order_, split=7, hooks=hooks.items(),
                  banks=(0, 1, 3))
            for n in range(8):
                bk, m = tile("w_out_2", H2, mixed)
                residual(n, nb, m, bk)
            prepare(cur[0] + 2)
            r = norm_r(nb)
            table("silu")
            (h,) = norm_apply(nb, r, [(H1H, H1L, cols("norm2_g_2", 8 * l, 8), None, plain)], w=(PE.last(),))
            barrier()
            lay.close()
            lay = ExitStack()
            nb = norm_bufs(lay, f"e{l}")
            ffn(f"d{l}", nb, lay, ("w_gate_2", "w_up_2", "w_down_2"), h, None, None)
            prepare(cur[0] + 2)
            r = norm_r(nb)
            if l == 0:
                rkeep = act(SG[:, :], nb["R"][:, :], w=(r,))
            else:
                for k in range(8):
                    t = stt(xk(k), xk(k), col("final_g_2", k), nb["R"][:, :], ALU.mult, ALU.mult, w=(r,))
                    SP.wait(t)
                    otk = s_out.sig(nc.sync.dma_start(out[128 * k:128 * k + 128, :], xk(k)))
            barrier()
            lay.close()
        SP.wait(otk, PE.last(), DVE.last(), SC.last(), PO.last())


def lay_out(inputs):
    parts = []
    for unit, _, tiles in plan():
        block = []
        for name, layer, k0, kn, n, nn in tiles:
            m = inputs[name] if layer is None else inputs[name][layer]
            if name == "pool_w_grp":
                m = m.reshape(1024, 256)
            b = m[128 * k0:128 * (k0 + kn), 128 * n:128 * (n + nn)]
            if unit == "ada":
                block.append(b.T)
            else:
                block.append(b.reshape(kn, 128, nn * 128).transpose(1, 0, 2).reshape(128, -1))
        parts.append(np.concatenate(block, axis=1).reshape(-1))
    stream = np.concatenate(parts)
    cols = np.concatenate([np.ascontiguousarray(inputs[n]).reshape(-1, 128).T for n, _ in COLS], axis=1)
    assert cols.shape == (128, NCOL)
    return stream, np.ascontiguousarray(inputs["c"][0]), np.ascontiguousarray(cols), np.ascontiguousarray(inputs["x"][0].T)


def kernel(**inputs):
    import concourse.bacc as _bacc
    from concourse.bass_utils import run_bass_kernel_spmd as _run

    ins = {k: np.asarray(v) for k, v in inputs.items()}
    stream, c, cols, xt = lay_out(ins)
    base, att, ret = tables()
    arrays = {"stream": stream, "c": c, "cols": cols, "xt": xt, "base": base, "att": att, "ret": ret}
    nc = _bacc.Bacc("TRN2", target_bir_lowering=False, num_devices=1, dynamic_dma_scratch_size=1024)
    args = [nc.dram_tensor(n, a.shape, F32, kind="ExternalInput").ap() for n, a in arrays.items()]
    y = nc.dram_tensor("y", (D, S), F32, kind="ExternalOutput").ap()
    program(nc, *args, y)
    r = _run(nc, [arrays], core_ids=[0])
    return np.ascontiguousarray(r.results[0]["y"].T).reshape(1, S, D)
```

```python
import math
from contextlib import ExitStack

import numpy as np
import concourse.bass as bass
from concourse import mybir

F32 = mybir.dt.float32
F32R = mybir.dt.float32r
ALU = mybir.AluOpType
ACT = mybir.ActivationFunctionType
AX_X = mybir.AxisListType.X

D, S, F, KC, FC, HC = 1024, 512, 2816, 8, 22, 11
NEG = -1.0e30
EPS = 1e-6
SLOT = 2048
WSLOT = HC * 128
GRP = 5

PAIR_TILES = [("w_kv", 0, "k"), ("attn_w_q", 0, "q"), ("w_kv", 1, "k"), ("attn_w_q", 1, "q"), ("w_kv", 2, "k"),
              ("attn_w_q", 2, "q"), ("w_kv", 0, "v"), ("w_kv", 1, "v"), ("w_kv", 2, "v")]
HEADS = [(kind, x) for x in range(4) for kind in "sr"]
HEAD_TILES = {"r": (("k", 4), ("q", 0), ("v", 8), ("g", 12)), "s": (("k", 20), ("q", 16), ("v", 24))}



def plan():
    def ada(name, layer, first, blocks):
        return [("ada", first + i, [(name, layer, 0, KC, b, 1) for b in blocks[i:i + 2]])
                for i in range(0, len(blocks), 2)]

    def pairs(tiles):
        return [("main", None, tiles[i:i + 2]) for i in range(0, len(tiles), 2)]

    def mix(main, side, n=1):
        out, side = [], list(side)
        for m in main:
            out.append(m)
            out += side[:n]
            side = side[n:]
        return out, side

    def square(name, layer, blocks):
        return [(name, layer, 0, KC, n, 1) for n in blocks]

    def ffn(gate, up, down, layer):
        out = []
        for half in range(2):
            for j in range(half * HC, half * HC + HC):
                out.append(("main", None, [(gate[0], layer, 0, KC, gate[1] + j, 1),
                                           (up[0], layer, 0, KC, up[1] + j, 1)]))
            out += [("main", None, [(down, layer, half * HC, HC, n, 1)]) for n in range(8)]
        return out

    units = []
    shift, scale = ada("ada_w", 0, 0, list(range(8))), ada("ada_w", 0, 8, list(range(8, 16)))
    for i in range(4):
        units += [shift[i], scale[i], ("main", None, [("pool_w_in", 0, 2 * i, 2, 8 - GRP, GRP)])]
    side = ada("ada_w", 0, 16, list(range(16, 48)))
    pool = pairs(square("pool_w_in", 0, range(8 - GRP)) + square("pool_w_grp", 0, range(2))
                 + square("pool_w_out", 0, range(8)))
    units += pool[:1]
    out, side = mix(pool[1:], side, 2)
    units += out
    side = side + ada("ada_w", 1, 48, list(range(48))) + ada("kv_ada_w", None, 96, list(range(16)))
    out, side = mix(ffn(("ffn_w_up", 0), ("ffn_w_up", FC), "ffn_w_down", 0), side)
    assert not side
    units += out
    qkv = []
    for p in range(8):
        for name, g, what in PAIR_TILES:
            qkv.append((name, 0 if what == "q" else None, 0, KC, (24 if what == "v" else 0) + 8 * g + p, 1))
    units += pairs(qkv)
    units += pairs(square("attn_w_o", 0, range(8)))
    units += ffn(("ffn_w_up", 0), ("ffn_w_up", FC), "ffn_w_down", 1)
    for l in range(2):
        w = []
        for kind, x in HEADS:
            w += square("w_in_2", l, [b + x for _, b in HEAD_TILES[kind]])
        units += pairs(w)
        units += pairs(square("w_out_2", l, range(8)))
        units += ffn(("w_gate_2", 0), ("w_up_2", 0), "w_down_2", l)
    return units


def words(tile):
    return tile[3] * tile[5] * 128


COLS = [("ada_b", 96), ("kv_ada_b", 16), ("norm1_g", 16), ("norm2_g", 16), ("pool_scale", 8),
        ("kv_norm_g", 8), ("final_g", 8), ("norm1_g_2", 16), ("norm2_g_2", 16), ("final_g_2", 8),
        ("ret_norm_g_2", 8), ("sb_norm_g_2", 8), ("ffn_conv_w", 132), ("ffn_conv_b", 44)]
COL = {}
NCOL = 0
for _n, _k in COLS:
    COL[_n] = NCOL
    NCOL += _k


def slopes():
    def pow2(m):
        start = 2.0 ** (-(2.0 ** -(math.log2(m) - 3)))
        return [start ** (i + 1) for i in range(m)]
    s = np.asarray(pow2(32) + pow2(64)[0::2][:16], dtype=np.float32)
    return (-np.sort(-s)).reshape(3, 16)


def tables():
    p = np.arange(128)[:, None]
    q = np.arange(128)[None, :]
    base = np.zeros((128, 704), np.float32)
    base[:, 0:128] = p == q
    base[:, 128:256] = 1.0
    base[:, 256:384] = -(p > q).astype(np.float32)
    base[:, 384:512] = -1.0
    base[:, 512:640] = p < q
    for g, w in enumerate((2, 4, 8, 16)):
        base[:, 640 + 16 * g:656 + 16 * g] = 1.0 / np.minimum(np.arange(16) + 1, w).astype(np.float32)[None, :]
    att = np.zeros((128, 1152), np.float32)
    for n in range(7):
        delta = 4 * (p - q) + (3 - n)
        att[:, 128 * n:128 * n + 128] = np.where((delta >= 0) & (delta <= 128), -delta, NEG)
    att[:, 896:1024] = np.where(p >= q, -4 * (p - q), NEG)
    att[:, 1024:1152] = np.where((p >= q) & ((p - q) % 4 == 0), -4 * (p - q), NEG)
    ret = np.zeros((128, 3072), np.float32)
    t = np.arange(512)[None, :]
    for h in range(4):
        lg = np.log1p(-np.exp2(-5.0 - h))
        w = np.exp(lg * np.abs(t - p)) * 128.0 ** -0.5
        ret[:, 512 * h:512 * h + 512] = np.where(t // 64 >= p // 64, w, 0.0)
    inv = (1.0 / (np.float32(10000.0) ** (np.arange(0, 128, 2, dtype=np.float32) / np.float32(128)))).astype(np.float32)
    ang = (np.arange(512, dtype=np.float32)[None, :] * inv[:, None]).astype(np.float32)
    ret[:, 2048:2560] = np.concatenate([np.cos(ang), np.cos(ang)])
    ret[:, 2560:3072] = np.concatenate([-np.sin(ang), np.sin(ang)])
    return base, att, ret


class Engine:

    def __init__(self, ns, sem):
        self.ns, self.sem, self.n, self.met = ns, sem, 0, {}

    def wait(self, *tokens):
        for t in tokens:
            if t is None:
                continue
            if isinstance(t, list):
                self.wait(*t)
                continue
            sem, value = t
            if self.met.get(id(sem), 0) < value:
                self.ns.wait_ge(sem, value)
                self.met[id(sem)] = value

    def sig(self, ins):
        ins.then_inc(self.sem, 1)
        self.n += 1
        return (self.sem, self.n)

    def last(self):
        return (self.sem, self.n)


class Slot:

    def __init__(self, sem):
        self.sem, self.n = sem, 0

    def sig(self, ins):
        ins.then_inc(self.sem, 16)
        self.n += 16
        return (self.sem, self.n)


def program(nc, stream, cd, colsd, xt, basd, attd, retd, out):
    units = plan()
    usize = [sum(words(t) for t in u[2]) for u in units]
    offs = np.concatenate([[0], np.cumsum([128 * n for n in usize])])
    tiles = [(u, j) for u, unit in enumerate(units) if unit[0] == "main" for j in range(len(unit[2]))]
    SL = slopes()
    top = ExitStack()
    with top:
        def sbuf(name, n, dt=F32, ctx=top):
            return ctx.enter_context(nc.sbuf_tensor(name, [128, n], dt))

        def sem(name):
            return top.enter_context(nc.semaphore(name))

        XT = sbuf("XT", 4096)
        H1H, H1L = sbuf("H1H", 4096, F32R), sbuf("H1L", 4096, F32R)
        RAW = [sbuf(f"RAW{i}", SLOT) for i in range(2)]
        WH = [sbuf(f"WH{i}", WSLOT, F32R) for i in range(3)]
        WL = [sbuf(f"WL{i}", WSLOT, F32R) for i in range(3)]
        SS, SG = sbuf("SS", 512), sbuf("SG", 512)
        CO = sbuf("CO", NCOL)
        MOD = sbuf("MOD", 112)
        AB = sbuf("AB", 40)
        KON = sbuf("KON", 2)
        BAS = sbuf("BAS", 704)
        PS = [top.enter_context(nc.psum_tensor(f"PS{i}", [128, 512], F32)) for i in range(8)]
        free = [None] * 8

        PE, DVE = Engine(nc.tensor, sem("pe")), Engine(nc.vector, sem("dve"))
        SC, PO = Engine(nc.scalar, sem("act")), Engine(nc.gpsimd, sem("pool"))
        SP = Engine(nc.sync, None)
        raw = [Slot(sem(f"raw{i}")) for i in range(2)]
        ara = [Slot(sem(f"ara{i}")) for i in range(3)]
        s_c, s_x, s_co, s_bas, s_att, s_ret = (Slot(sem(n)) for n in ("d_c", "d_x", "d_co", "d_bas", "d_att", "d_ret"))
        s_out = Slot(sem("d_out"))

        IDENT, ONES, UNEG, NONES = (BAS[:, 128 * i:128 * i + 128] for i in range(4))
        STRICT = BAS[:, 512:640]
        ONE, EPSC = KON[:, 0:1], KON[:, 1:2]
        top.enter_context(nc.Block())

        def chunk(buf, k):
            return buf[:, 512 * k:512 * k + 512]

        def xk(k):
            return chunk(XT, k)

        def cols(name, i, n):
            return CO[:, COL[name] + i:COL[name] + i + n]

        def col(name, i):
            return cols(name, i, 1)

        def act(out_, in_, fn=ACT.Copy, w=(), **kw):
            SC.wait(*w)
            return SC.sig(nc.scalar.activation(out_, in_, fn, **kw))

        def tt(out_, a, b, op, w=(), e=None):
            e = e or DVE
            e.wait(*w)
            return e.sig(e.ns.tensor_tensor(out_, a, b, op))

        def stt(out_, a, s, b, op0, op1, w=()):
            DVE.wait(*w)
            return DVE.sig(nc.vector.scalar_tensor_tensor(out_, a, s, b, op0, op1))

        def ts(out_, a, s1, s2, op0, op1=None, w=()):
            DVE.wait(*w)
            if op1 is None:
                return DVE.sig(nc.vector.tensor_scalar(out_, a, s1, None, op0))
            return DVE.sig(nc.vector.tensor_scalar(out_, a, s1, s2, op0, op1))

        def mms(items, w=()):
            PE.wait(*w)
            for it in items:
                if len(it) > 5:
                    PE.wait(it[5])
                ins = nc.tensor.matmul(it[0], it[1], it[2], start=it[3], stop=it[4], skip_group_check=True)
            return PE.sig(ins)

        def turn4(bk, srcs, w):
            PE.wait(*w, free[bk], bastok)
            for n, src in enumerate(srcs):
                ins = nc.tensor.transpose(PS[bk][:, 128 * n:128 * n + 128], src, IDENT)
            return PE.sig(ins)

        def table(name):
            nc.scalar.preload_act_table_set(name + "_and_others")

        nload = [0]
        order = {"main": 0, "ada": 0}
        place, loaded, ready_at = {}, {}, {}
        rawfree, arafree = [None, None], [None] * 3
        nunit, ntile = [0], [0]
        wfree = [None] * 3
        wtok = {}
        usepool = [False]
        ahead = [0]
        AR, condtok, modtok = [], [None], [None]

        def load():
            while nload[0] < len(units):
                u = nload[0]
                kind = units[u][0]
                n = order[kind]
                ring = 2 if kind == "main" else 3
                if n >= ring and not ready_at.get((kind, n - ring)):
                    return
                i = n % ring
                place[u] = i
                SP.wait((rawfree if kind == "main" else arafree)[i])
                src = stream[int(offs[u]):int(offs[u + 1])].rearrange("(p n) -> p n", p=128)
                dst = (RAW if kind == "main" else AR)[i]
                slot = (raw if kind == "main" else ara)[i]
                loaded[u] = slot.sig(nc.sync.dma_start(dst[:, 0:usize[u]], src))
                order[kind] += 1
                nload[0] += 1

        seen = {"main": 0, "ada": 0}

        def finished(kind):
            ready_at[(kind, seen[kind])] = True
            seen[kind] += 1
            load()

        def ada_unit(u):
            i = place[u]
            first = units[u][1]
            for q in range(2):
                src = AR[i][:, 1024 * q:1024 * q + 1024]
                bias = col("ada_b", first + q) if first < 96 else col("kv_ada_b", first - 96 + q)
                DVE.wait(loaded[u], condtok[0], cotok)
                t = DVE.sig(nc.vector.tensor_tensor_reduce(src, src, COND[:, :], 1.0, bias, ALU.mult, ALU.add,
                                                           MOD[:, first + q:first + q + 1]))
            arafree[i] = modtok[0] = t
            finished("ada")

        def prepare(t):
            while ntile[0] <= t and ntile[0] < len(tiles):
                u, j = tiles[ntile[0]]
                while nunit[0] < u:
                    if units[nunit[0]][0] == "ada":
                        ada_unit(nunit[0])
                    nunit[0] += 1
                spec = units[u][2][j]
                base = sum(words(x) for x in units[u][2][:j])
                n, i, s = words(spec), place[u], ntile[0] % 3
                src = RAW[i][:, base:base + n]
                hi = act(WH[s][:, 0:n], src, w=(loaded[u], wfree[s]))
                e = PO if usepool[0] else DVE
                lo = tt(WL[s][:, 0:n], src, WH[s][:, 0:n].bitcast(F32), ALU.subtract, w=(hi, loaded[u], wfree[s]),
                        e=e)
                wtok[ntile[0]] = lo
                if j == len(units[u][2]) - 1:
                    rawfree[i] = lo
                    nunit[0] = u + 1
                    finished("main")
                ntile[0] += 1

        cur = [0]

        def take(name):
            t = cur[0]
            cur[0] += 1
            u, j = tiles[t]
            assert units[u][2][j][0] == name, (name, units[u][2][j])
            prepare(t)
            prepare(t + ahead[0])
            return t % 3, wtok[t], units[u][2][j]

        ring = [0]
        ALLB = (0, 1, 2, 3, 4, 5, 6)

        def bank(banks=ALLB):
            ring[0] += 1
            return banks[ring[0] % len(banks)]

        def three(bank_ap, s, o, hi, lo, first, last, rt=None):
            wh, wl = WH[s][:, o:o + 128], WL[s][:, o:o + 128]
            return [(bank_ap, wh, hi, first, False, rt), (bank_ap, wh, lo, False, False),
                    (bank_ap, wl, hi, False, last)]

        early_tiles = []

        def tile(name, hl, ready=None, banks=ALLB, middle=None):
            if early_tiles:
                t, bk, m = early_tiles.pop(0)
                prepare(t + ahead[0])
                for k in (2, 4) if middle else ():
                    middle(k)
                return bk, m
            s, tok, spec = take(name)
            bk = bank(banks)
            hi, lo = hl
            items = []
            for k in range(spec[3]):
                if k in (2, 4) and middle:
                    mms(items, w=(tok, free[bk]))
                    items = []
                    middle(k)
                items += three(PS[bk][:, :], s, 128 * k, chunk(hi, k), chunk(lo, k), k == 0, k == spec[3] - 1,
                               ready[k] if ready else None)
            m = mms(items, w=(tok, free[bk]))
            wfree[s] = m
            return bk, m

        def group(names, hls, readys, korder=tuple(range(8)), split=4, hooks=(), banks=ALLB):
            t0 = cur[0]
            hooks = dict(hooks)
            prepare(t0 + len(names) - 1)
            got = []
            for n in names:
                t = cur[0]
                cur[0] += 1
                u, j = tiles[t]
                assert units[u][2][j][0] == n
                got.append((t, bank(banks)))
            toks = []

            def part(x, ks):
                t, bk = got[x]
                items = []
                for k in ks:
                    items += three(PS[bk][:, :], t % 3, 128 * k, chunk(hls[x][0], k), chunk(hls[x][1], k),
                                   k == korder[0], k == korder[-1], readys[x][k] if readys[x] else None)
                return mms(items, w=(wtok[t], free[bk]))

            for n, k in enumerate(korder[:split]):
                for x in range(len(names)):
                    part(x, [k])
                    if 3 * n + x in hooks:
                        hooks[3 * n + x]()
            for x in range(len(names)):
                m = part(x, korder[split:])
                wfree[got[x][0] % 3] = m
                early_tiles.append((got[x][0], got[x][1], m))
                prepare(t0 + 3 + x)

        def barrier(*others):
            toks = [e.last() for e in (PE, DVE, SC, PO) if e.n]
            for e in (DVE, SC, PO, *others):
                e.wait(*toks)

        ssa, sga = [None], [None]
        sq7 = [None]

        def norm_bufs(ctx, tag):
            names = ["SQ0", "SQ1", "R", "T0", "T1", "T2", "V0", "V1", "V2", "V3"]
            b = {n: sbuf(n + tag, 512, F32, ctx) for n in names}
            b.update(SQ=[b["SQ0"], b["SQ1"]], T=[b["T0"], b["T1"], b["T2"]], V=[b["V0"], b["V1"], b["V2"], b["V3"]],
                     sq=[None, None], tf=[None] * 3, vf=[None] * 4, n=0)
            return b

        def add_square(b, k, w, acc=None, state=None, scale=1.0):
            acc, state = acc or SS, state or ssa
            if k == 0:
                state[0] = act(acc[:, :], xk(0), ACT.Square, scale=scale, w=(w, state[0]))
                return
            i = b["n"] % 2 if k < 7 or acc is SG else 1
            b["n"] = i + 1
            t = act(b["SQ"][i][:, :], xk(k), ACT.Square, scale=scale, w=(w, b["sq"][i]))
            if k == 7 and acc is SS:
                sq7[0] = b["sq"][1] = t
                return
            state[0] = b["sq"][i] = tt(acc[:, :], acc[:, :], b["SQ"][i][:, :], ALU.add, w=(t, state[0]))

        def rsqrt_of(bk, out_, scale, w):
            t = free[bk] = act(out_, PS[bk][:, :], ACT.Ln, bias=EPSC, scale=scale, w=(*w, kontok))
            return act(out_, out_, ACT.Exp, scale=-0.5, w=(t,))

        def norm_r(b, out_=None, w=()):
            i = bank()
            mms([(PS[i][:, :], ONES, SS[:, :], True, False)], w=(ssa[0], free[i], bastok))
            m = mms([(PS[i][:, :], ONES, b["SQ"][1][:, :], False, True)], w=(sq7[0],))
            ssa[0] = b["sq"][1] = m
            return rsqrt_of(i, out_ or b["R"][:, :], 1.0 / D, (m, *w))

        def norm_k(b, r, k, outs, w=()):
            i = k % 3
            t = tt(b["T"][i][:, :], xk(k), b["R"][:, :], ALU.mult, w=(r, *w, b["tf"][i]))
            used, got = [], []
            for n, (hi, lo, gain, shift, view) in enumerate(outs):
                j = (k * len(outs) + n) % 4
                v = b["V"][j]
                if n == 0:
                    t2 = act(v[:, :], b["T"][i][:, :], ACT.Identity, scale=gain[:, k:k + 1], bias=shift[:, k:k + 1],
                             w=(t, b["vf"][j], *w))
                else:
                    t2 = ts(v[:, :], b["T"][i][:, :], gain[:, k:k + 1], shift[:, k:k + 1], ALU.mult, ALU.add,
                            w=(t, b["vf"][j]))
                used.append(t2)
                got.append((j, t2))
            b["tf"][i] = used
            return got

        def norm_split(b, k, outs, got):
            toks = []
            for n, (hi, lo, gain, shift, view) in enumerate(outs):
                j, t2 = got[n]
                v = b["V"][j]
                h = act(view(chunk(hi, k)), v[:, :], w=(t2,))
                pool = (n == 0) if len(outs) > 1 else (k % 2 == 1)
                l = tt(view(chunk(lo, k)), v[:, :], view(chunk(hi, k)).bitcast(F32), ALU.subtract, w=(t2, h),
                       e=PO if pool else DVE)
                b["vf"][j] = l
                toks.append(l)
            return toks

        def norm_apply(b, r, outs, w=(), ks=tuple(range(8))):
            got, toks = norm_k(b, r, ks[0], outs, w), []
            for k in ks:
                nxt = norm_k(b, r, k + 1, outs, w) if k != ks[-1] and k else None
                toks.append(norm_split(b, k, outs, got))
                if k != ks[-1]:
                    got = nxt or norm_k(b, r, k + 1, outs, w)
            return [[g[n] for g in toks] for n in range(len(outs))]

        def split_x(k, gain, w):
            h = act(chunk(H1H, k), xk(k), scale=gain[:, k:k + 1], w=w)
            return stt(chunk(H1L, k), xk(k), gain[:, k:k + 1], chunk(H1H, k).bitcast(F32), ALU.mult, ALU.subtract,
                       w=(h, *w))

        def plain(ap):
            return ap

        def permuted(ap):
            return ap.rearrange("p (r j) -> p j r", r=4)

        def mod(first, n=8):
            return MOD[:, first:first + n]

        def gains(at, name, i, scale_col, n=8):
            return stt(AB[:, at:at + n], mod(scale_col, n), 1.0, cols(name, i, n), ALU.add, ALU.mult,
                       w=(modtok[0], cotok))

        def residual(n, b, m, bk, gcol=None, square=True, second=False):
            if gcol is None:
                t = tt(xk(n), PS[bk][:, :], xk(n), ALU.add, w=(m,))
            else:
                t = stt(xk(n), PS[bk][:, :], gcol, xk(n), ALU.mult, ALU.add, w=(m,))
            free[bk] = t
            if square:
                add_square(b, n, t)
                if second:
                    add_square(b, n, t, SG, sga, col("final_g", n))
            return t

        def split_out(bk, hi, lo, m, scale, w=()):
            h = act(hi, PS[bk][:, :], scale=scale, w=(m, *w))
            l = stt(lo, PS[bk][:, :], scale, hi.bitcast(F32), ALU.mult, ALU.subtract, w=(h,))
            free[bk] = l
            return l

        H1 = (H1H, H1L)

        early = ExitStack()
        AR += [sbuf(f"AR{i}", SLOT, F32, early) for i in range(3)]
        COND = sbuf("COND", 1024, F32, early)
        nb = norm_bufs(early, "a")
        table("silu")
        ctok = s_c.sig(nc.scalar.dma_start(COND[:, :], cd.partition_broadcast(128)))
        cotok = s_co.sig(nc.sync.dma_start(CO[:, :], colsd))
        xtok = s_x.sig(nc.sync.dma_start(XT[:, :].rearrange("p (k t) -> p k t", k=8),
                                         xt.rearrange("(k p) t -> p k t", p=128)))
        bastok = s_bas.sig(nc.sync.dma_start(BAS[:, :], basd))
        load()
        PO.sig(nc.gpsimd.memset(ONE, 1.0))
        kontok = PO.sig(nc.gpsimd.memset(EPSC, EPS))
        condtok[0] = act(COND[:, :], COND[:, :], ACT.Silu, w=(ctok,))
        table("natural_log_exp")
        for k in range(8):
            add_square(nb, k, xtok)
        r = norm_r(nb)
        usepool[0] = True
        h1 = []
        kb = [0, 1, 2, 3, 4]
        for i in range(4):
            s, tok, spec = take("pool_w_in")
            ta = gains(2 * i, "norm1_g", 2 * i, 8 + 2 * i, 2)
            h1 += norm_apply(nb, r, [(H1H, H1L, AB[:, 0:8], mod(0), plain)], w=(ta,), ks=(2 * i, 2 * i + 1))[0]
            for j in range(2):
                for x in range(GRP):
                    k = 2 * i + j
                    m = mms(three(PS[kb[x]][:, :], s, 128 * (GRP * j + x), chunk(H1H, k), chunk(H1L, k),
                                  k == 0, k == 7, h1[k]), w=(tok, free[kb[x]]))
            wfree[s] = m
            if i < 3:
                prepare(cur[0])
        ahead[0] = 2
        prepare(cur[0] + 1)

        pool = ExitStack()
        H2H, H2L = sbuf("H2Ha", 4096, F32R, pool), sbuf("H2La", 4096, F32R, pool)
        U = [sbuf(f"U{i}", 528, F32, pool) for i in range(2)]
        V = [[sbuf(f"V{i}{j}", 528, F32, pool) for i in range(2)] for j in range(2)]
        tz = None
        for t_ in (*U, *V[0], *V[1]):
            tz = DVE.sig(nc.vector.memset(t_[:, 0:16], 0.0))
        ufree, vfree, h2 = [None, None], [None, None], [None] * 8

        pend = []

        def pooled(n, bk, m):
            g, i = n // 2, pcount[0] % 2
            pcount[0] += 1
            u = U[i]
            t = free[bk] = act(u[:, 16:528], PS[bk][:, :], w=(m, ufree[i], tz))
            src, sh, dst = u, 1, 0
            DVE.wait(vfree[i])
            for _ in range(g + 1):
                d = V[i][dst]
                t = tt(d[:, 16:528], src[:, 16:528], src[:, 16 - sh:528 - sh], ALU.add, w=(t, tz))
                src, sh, dst = d, sh * 2, 1 - dst
            p = V[i][dst]
            t1 = stt(p[:, 16:528], src[:, 16:528], 1.0 / sh, u[:, 16:528], ALU.mult, ALU.subtract, w=(t,))
            t2 = tt(p[:, 16:16 + sh], src[:, 16:16 + sh], BAS[:, 640 + 16 * g:640 + 16 * g + sh], ALU.mult,
                    w=(t1, bastok))
            t3 = tt(p[:, 16:16 + sh], p[:, 16:16 + sh], u[:, 16:16 + sh], ALU.subtract, w=(t2,))
            ufree[i] = t3
            pend.append((n, i, p, t3))

        def pooled_split():
            n, i, p, t3 = pend.pop(0)
            hh = act(chunk(H2H, n), p[:, 16:528], w=(t3,))
            h2[n] = vfree[i] = tt(chunk(H2L, n), p[:, 16:528], chunk(H2H, n).bitcast(F32), ALU.subtract,
                                  w=(t3, hh), e=PO)

        pcount = [0]
        pooled(3, kb[0], m)
        pooled(4, kb[1], m)
        pooled_split()
        for n in range(8 - GRP):
            bk, mt = tile("pool_w_in", H1, h1, banks=(5, 6))
            for _ in range(2):
                x = pcount[0]
                if x < GRP:
                    pooled(8 - GRP + x, kb[x], m)
                    pooled_split()
            last = (n, bk, mt)
            if n:
                pooled(*before)
                pooled_split()
            before = last
        pooled(*before)
        while pend:
            pooled_split()
        gfree = PE.last()
        h1 = [None] * 8
        for d in range(2):
            s, tok, _ = take("pool_w_grp")
            for g in (3, 2, 0, 1):
                bk = bank()
                items = []
                for i in range(2):
                    c = 2 * g + i
                    items += three(PS[bk][:, :], s, 128 * c, chunk(H2H, c), chunk(H2L, c), i == 0, i == 1, h2[c])
                m = mms(items, w=(tok, free[bk]))
                n = 2 * g + d
                h1[n] = split_out(bk, chunk(H1H, n), chunk(H1L, n), m, col("pool_scale", n), w=(gfree,))
            wfree[s] = m
        for n in range(8):
            bk, m = tile("pool_w_out", H1, h1)
            residual(n, nb, m, bk, MOD[:, 16 + n:17 + n])
        pool.close()
        barrier()

        def ffn(tag, b, ctx, names, h, conv, gate, second=False, factor=None, gain=None):
            GH, GL = sbuf(f"GH{tag}", HC * 512, F32R, ctx), sbuf(f"GL{tag}", HC * 512, F32R, ctx)
            Y = [sbuf(f"Y{tag}{i}", 512, F32, ctx) for i in range(2)]
            SI = [sbuf(f"SI{tag}{i}", 512, F32, ctx) for i in range(2)]
            gfree = None
            gt = [None, None]
            na, nv, nd = names
            hx = []
            if factor is None:
                group([na, nv, na], [H1] * 3, [h] * 3)
            for half in range(2):
                ready = []
                for jj in range(HC):
                    j, i = half * HC + jj, jj % 2
                    ba, ma = tile(na, H1, h)
                    if conv is not None:
                        cw = [col("ffn_conv_w", conv * 66 + q * 22 + j) for q in range(3)]
                        y = act(Y[i][:, :], PS[ba][:, :], ACT.Identity, scale=cw[2],
                                bias=col("ffn_conv_b", conv * 22 + j), w=(ma, gt[i]))
                        y = stt(Y[i][:, 1:512], PS[ba][:, 0:511], cw[1], Y[i][:, 1:512], ALU.mult, ALU.add, w=(y,))
                        y = stt(Y[i][:, 2:512], PS[ba][:, 0:510], cw[0], Y[i][:, 2:512], ALU.mult, ALU.add, w=(y,))
                        free[ba] = y
                        si = act(SI[i][:, :], Y[i][:, :], ACT.Silu, w=(y,))
                    else:
                        si = free[ba] = tt(SI[i][:, :], PS[ba][:, :], SG[:, :], ALU.mult, w=(ma, gt[i], factor))
                        si = act(SI[i][:, :], SI[i][:, :], ACT.Silu, w=(si,))
                        si = tt(SI[i][:, :], SI[i][:, :], SG[:, :], ALU.mult, w=(si, factor), e=PO)
                    bv, mv = tile(nv, H1, h)
                    g = free[bv] = tt(SI[i][:, :], SI[i][:, :], PS[bv][:, :], ALU.mult, w=(mv, si))
                    g1 = act(chunk(GH, jj), SI[i][:, :], w=(g, gfree))
                    g2 = tt(chunk(GL, jj), SI[i][:, :], chunk(GH, jj).bitcast(F32), ALU.subtract, w=(g1,))
                    gt[i] = g2
                    ready.append(g2)
                if half:
                    table("natural_log_exp")
                    hfree = PE.last()
                for n in range(8):
                    bk, m = tile(nd, (GH, GL), ready)
                    gfree = m
                    t = residual(n, b, m, bk, None if gate is None else MOD[:, gate + n:gate + n + 1],
                                 square=half == 1, second=second)
                    if half and gain is not None:
                        hx.append(split_x(n, gain, (t, hfree)))
            return hx

        prepare(cur[0] + 2)
        ta = gains(8, "norm2_g", 0, 32)
        r = norm_r(nb)
        table("silu")
        (h,) = norm_apply(nb, r, [(H1H, H1L, AB[:, 8:16], mod(24), plain)], w=(ta, PE.last()))
        ffn("a", nb, early, ("ffn_w_up", "ffn_w_up", "ffn_w_down"), h, 0, 40)
        usepool[0] = False
        prepare(cur[0] + 2)
        ta1 = gains(16, "norm1_g", 8, 48 + 8)
        takv = gains(24, "kv_norm_g", 0, 96 + 8)
        gains(32, "norm2_g", 8, 48 + 32)
        r = norm_r(nb)
        rsave = act(SG[:, :], nb["R"][:, :], w=(r,))
        early.close()
        barrier()

        att = ExitStack()
        H2H, H2L = sbuf("H2Hb", 4096, F32R, att), sbuf("H2Lb", 4096, F32R, att)
        H2 = (H2H, H2L)
        ATT = sbuf("ATT", 1152, F32, att)
        QT = [sbuf(f"QT{i}", 1536, F32, att) for i in range(2)]
        KT = [sbuf(f"KT{i}", 1536, F32, att) for i in range(2)]
        VV = [sbuf(f"VV{i}", 1536, F32, att) for i in range(2)]
        OT = sbuf("OT", 4096, F32, att)
        VF = sbuf("VF", 512, F32, att)
        STAT = sbuf("STAT", 16, F32, att)
        sub = ExitStack()
        nb = norm_bufs(sub, "b")
        nb["R"] = SG
        hq, hkv = norm_apply(nb, rsave, [(H1H, H1L, AB[:, 16:24], mod(48), permuted),
                                         (H2H, H2L, AB[:, 24:32], mod(96), permuted)], w=(ta1, takv, PE.last()))
        SP.wait(PE.last(), DVE.last(), SC.last(), PO.last())
        atok = s_att.sig(nc.sync.dma_start(ATT[:, :], attd))
        subtok = [DVE.last(), SC.last(), PO.last()]
        sub.close()
        SB = [sbuf(f"SB{i}", 1536, F32, att) for i in range(2)]
        PT = [sbuf(f"PT{i}", 1536, F32, att) for i in range(2)]

        used, vtok, defer = {}, [None], []
        qkvtok = {}
        group(["w_kv", "attn_w_q", "w_kv"], [H2, H1, H2], [hkv, hq, hkv], banks=(0, 1, 2))

        def project(t):
            p, x = t // 9, t % 9
            i = p % 2
            name, g, what = PAIR_TILES[x]

            def middle(k):
                while defer and k == 2:
                    defer.pop(0)()
                run_events(t + k / 8)

            bk, m = tile(name, H1 if what == "q" else H2, banks=(0, 1), middle=middle)
            if what == "v":
                tv = free[bk] = act(VF[:, :], PS[bk][:, :], w=(m, vtok[0]))

                def rest():
                    m2 = vtok[0] = turn4(5, [VF[:, 128 * q:128 * q + 128] for q in range(4)], (tv,))
                    qkvtok[p] = free[5] = act(chunk(VV[i], g), PS[5][:, :], w=(m2, used.get(p - 2)))
                defer.append(rest)
            else:
                dst = (QT if what == "q" else KT)[i]
                qkvtok[p] = free[bk] = act(chunk(dst, g), PS[bk][:, :], scale=0.125 if what == "q" else 1.0,
                                           w=(m, used.get(p - 2)))

        sbfree, ptfree = [subtok, subtok], [subtok, subtok]
        stok, ttok, otok = {}, {}, {}

        def scores(p, r_):
            i, n = p % 2, (4 * p + r_) % 2
            sb = SB[n]
            tok = []
            for hh in range(2):
                head = 2 * p + hh
                po = slice(64 * hh, 64 * hh + 64)
                q = [QT[i][po, 512 * g + 128 * r_:512 * g + 128 * r_ + 128] for g in range(3)]
                m0 = mms([(PS[2 + hh][:, :], q[0], KT[i][po, 0:512], True, True)], w=(free[2 + hh], qkvtok[p]))
                m1 = mms([(PS[4][:, 256 * hh + 128 * g - 128:256 * hh + 128 * g], q[g],
                           KT[i][po, 512 * g + 128 * r_:512 * g + 128 * r_ + 128], hh == 0 and g == 1, True)
                          for g in (1, 2)], w=(free[4],) if hh == 0 else (tok[0][1],))
                tok.append((m0, m1))
            for hh in range(2):
                head = 2 * p + hh
                m0, m1 = tok[hh]
                o = 768 * hh
                free[2 + hh] = stt(sb[:, o:o + 512], ATT[:, 128 * (3 - r_):128 * (3 - r_) + 512],
                                   float(SL[0][head]), PS[2 + hh][:, :], ALU.mult, ALU.add,
                                   w=(m0, sbfree[n], atok))
                DVE.wait(tok[1][1])
                for g in (1, 2):
                    t1 = stt(sb[:, o + 384 + 128 * g:o + 512 + 128 * g], ATT[:, 768 + 128 * g:896 + 128 * g],
                             float(SL[g][head]), PS[4][:, 256 * hh + 128 * g - 128:256 * hh + 128 * g],
                             ALU.mult, ALU.add)
                z = 8 * n + 4 * hh
                DVE.wait(t1)
                t2 = DVE.sig(nc.vector.tensor_reduce(STAT[:, z:z + 1], sb[:, o:o + 768], AX_X, ALU.max))
                t3 = ts(STAT[:, z + 1:z + 2], STAT[:, z:z + 1], -1.0, None, ALU.mult, w=(t2,))
                stok[(p, r_, hh)] = act(sb[:, o:o + 768], sb[:, o:o + 768], ACT.Exp, bias=STAT[:, z + 1:z + 2],
                                        scale=1.0, accum_out=STAT[:, z + 2:z + 3], w=(t3,))
            free[4] = t1

        def norms(p, r_):
            n = (4 * p + r_) % 2
            for hh in range(2):
                z, o = 8 * n + 4 * hh, 768 * hh
                DVE.wait(stok[(p, r_, hh)])
                t = DVE.sig(nc.vector.reciprocal(STAT[:, z + 3:z + 4], STAT[:, z + 2:z + 3]))
                stok[(p, r_, hh)] = ts(SB[n][:, o:o + 768], SB[n][:, o:o + 768], STAT[:, z + 3:z + 4], None,
                                       ALU.mult, w=(t,))

        def transposes(p, r_):
            n = (4 * p + r_) % 2
            sb, pt = SB[n], PT[n]
            got = ttok[(p, r_)] = []

            def third(c):
                bk = 6 + (3 * (4 * p + r_) + c) % 2 if p < 7 else 7
                m = turn4(bk, [sb[:, 512 * c + 128 * q:512 * c + 128 * q + 128] for q in range(4)],
                          (stok[(p, r_, 0)], stok[(p, r_, 1)]))
                if c == 1:
                    DVE.wait(m, ptfree[n])
                    t = DVE.sig(nc.vector.tensor_copy(chunk(pt, c), PS[bk][:, :]))
                else:
                    t = act(chunk(pt, c), PS[bk][:, :], w=(m, ptfree[n]))
                free[bk] = t
                got.append(t)
                sbfree[n] = m

            third(0)
            if p < 7:
                third(1)
            else:
                defer.append(lambda: third(1))
            defer.append(lambda: third(2))

        def values(p, r_):
            i, n = p % 2, (4 * p + r_) % 2
            pt = PT[n]
            PE.wait(ttok[(p, r_)], free[5])
            for c in range(6):
                g, kt = (0, c) if c < 4 else (c - 3, r_)
                for hh in range(2):
                    v = VV[i][:, 512 * g + 128 * kt + 64 * hh:512 * g + 128 * kt + 64 * hh + 64]
                    ins = nc.tensor.matmul(PS[5][64 * hh:64 * hh + 64, 0:128], v,
                                           pt[:, 768 * hh + 128 * c:768 * hh + 128 * c + 128],
                                           start=c == 0, stop=c == 5, skip_group_check=True)
            m = ptfree[n] = PE.sig(ins)
            if r_ == 3:
                used[p] = m
            free[5] = otok[p] = act(OT[:, 512 * p + 128 * r_:512 * p + 128 * r_ + 128], PS[5][:, 0:128], w=(m,))

        events = []
        for g in range(32):
            at = 9 * (g // 4 + 1) + (0, 2, 4, 7)[g % 4]
            events += [(at + 0.1, g, scores), (at + 1.5, g, norms), (at + 2, g, transposes), (at + 3, g, values)]
        events.sort(key=lambda e: (e[0], e[1]))

        def run_events(until):
            while events and events[0][0] <= until + 0.1:
                _, g, fn = events.pop(0)
                fn(g // 4, g % 4)

        for t in range(72):
            run_events(t)
            project(t)
        while defer:
            defer.pop(0)()
        hfree = PE.last()
        oready = [None] * 8

        def natural(ap):
            return ap.rearrange("p (j r) -> p j r", r=4)

        def out_split(k, e):
            src = chunk(OT, k).rearrange("p (r j) -> p j r", r=4)
            t = act(natural(chunk(H1H, k)), src, w=(otok[k], hfree))
            oready[k] = tt(natural(chunk(H1L, k)), src, natural(chunk(H1H, k).bitcast(F32)), ALU.subtract,
                           w=(t, otok[k], hfree), e=e)

        run_events(72)
        while defer:
            defer.pop(0)()
        for k in range(6):
            out_split(k, PO if k % 2 else DVE)

        def last_of_six(p, r_):
            values(6, 3)
            out_split(6, DVE)

        steps = [(3, last_of_six), (0, norms), (1, scores), (1, norms), (0, transposes), (0, None), (0, None), (2, scores),
                 (0, values), (2, norms), (1, transposes), (1, None), (1, None), (3, scores), (1, values),
                 (3, norms), (2, transposes), (2, None), (2, None), (2, values), (3, transposes), (3, None),
                 (3, None), (3, values)]
        events.clear()

        def step():
            r_, fn = steps.pop(0)
            if fn is None:
                defer.pop(0)()
            else:
                fn(7, r_)

        def hook():
            step()

        def last_hook():
            while steps:
                step()
            out_split(7, DVE)

        group(["attn_w_o"] * 3, [H1] * 3, [oready] * 3, split=7, hooks=[(n, hook if n < 20 else last_hook) for n in range(21)],
              banks=(0, 1, 6))
        barrier()
        att.close()

        lay = ExitStack()
        nb = norm_bufs(lay, "c")
        for n in range(8):
            bk, m = tile("attn_w_o", H1, oready)
            residual(n, nb, m, bk, MOD[:, 64 + n:65 + n])
        prepare(cur[0] + 2)
        r = norm_r(nb)
        table("silu")
        (h,) = norm_apply(nb, r, [(H1H, H1L, AB[:, 32:40], mod(48 + 24), plain)], w=(PE.last(),))
        tg = tt(AB[:, 0:8], cols("final_g", 0, 8), cols("norm1_g_2", 0, 8), ALU.mult)
        SC.wait(tg)
        DVE.wait(tg)
        hx = ffn("b", nb, lay, ("ffn_w_up", "ffn_w_up", "ffn_w_down"), h, 1, 48 + 40, second=True, gain=AB[:, 0:8])
        prepare(cur[0] + 2)
        r = norm_r(nb, SS[:, :])
        i = bank()
        m = mms([(PS[i][:, :], ONES, SG[:, :], True, True)], w=(sga[0], free[i]))
        T0 = nb["T"][0]
        t = tt(T0[:, :], SS[:, :], PS[i][:, :], ALU.mult, w=(r, m))
        free[i] = t
        t = tt(T0[:, :], T0[:, :], SS[:, :], ALU.mult, w=(t,))
        t = act(T0[:, :], T0[:, :], ACT.Ln, bias=EPSC, scale=1.0 / D, w=(t,))
        t = act(T0[:, :], T0[:, :], ACT.Exp, scale=-0.5, w=(t,))
        factor = tt(SG[:, :], T0[:, :], SS[:, :], ALU.mult, w=(t, m, r))
        barrier()
        lay.close()

        for l in range(2):
            lay = ExitStack()
            H2H, H2L = sbuf(f"H2Hc{l}", 4096, F32R, lay), sbuf(f"H2Lc{l}", 4096, F32R, lay)
            H2 = (H2H, H2L)
            nb = norm_bufs(lay, f"d{l}")
            RT = sbuf(f"RT{l}", 3072, F32, lay)
            DEC = [RT[:, 512 * i:512 * i + 512] for i in range(4)]
            COS, SIN = RT[:, 2048:2560], RT[:, 2560:3072]
            Q = [sbuf(f"Q{l}{i}", 512, F32, lay) for i in range(3)]
            K = [sbuf(f"K{l}{i}", 512, F32, lay) for i in range(3)]
            G = [sbuf(f"G{l}{i}", 512, F32, lay) for i in range(2)]
            W = [sbuf(f"W{l}{i}", 512, F32, lay) for i in range(3)]
            VR = sbuf(f"VR{l}", 512, F32, lay)
            TMP = [sbuf(f"TMP{l}{i}", 512, F32, lay) for i in range(2)]
            AA = sbuf(f"AA{l}", 1280, F32, lay)
            SPL = sbuf(f"SPL{l}", 1280, F32, lay)
            OBS = [sbuf(f"OB{l}{i}", 512, F32, lay) for i in range(2)]
            OCS = [sbuf(f"OC{l}{i}", 512, F32, lay) for i in range(2)]
            SP.wait(PE.last(), DVE.last(), SC.last(), PO.last())
            rtok = s_ret.sig(nc.sync.dma_start(RT[:, :], retd))
            tok = {}
            tmpfree = {"k": None, "q": None}
            OFF = [0, 512, 896, 1152]
            WID = [512, 384, 256, 128]
            SBK = [(2, 0), (3, 0), (4, 0), (3, 384)]
            LBK = [(5, 0), (6, 0), (7, 0), (6, 384)]
            mixed = [None] * 8
            defer = []
            jobs = [(n, what) for n in range(8) for what, _ in HEAD_TILES[HEADS[n][0]]]

            def proj(t_):
                n, what = jobs[t_]
                kind, x = HEADS[n]
                i = n % 3
                done = tok.get(("used", n - 3))
                bk, m = tile("w_in_2", H1, hx, banks=(0, 1))
                while defer:
                    defer.pop(0)()
                if what in "kq" and kind == "r":
                    dst = (K if what == "k" else Q)[i]
                    tp = TMP[0 if what == "k" else 1]
                    s1 = act(tp[0:64, :], PS[bk][64:128, :], w=(m, tmpfree[what]))
                    s2 = act(tp[64:128, :], PS[bk][0:64, :])
                    c1 = free[bk] = tt(dst[:, :], PS[bk][:, :], COS, ALU.mult, w=(s2, done, turned))
                    c2 = tt(tp[:, :], tp[:, :], SIN, ALU.mult, w=(s1, s2, turned), e=PO)
                    t = tmpfree[what] = tt(dst[:, :], dst[:, :], tp[:, :], ALU.add, w=(c1, c2), e=PO)
                elif what in "kq":
                    dst = (K if what == "k" else Q)[i]
                    t = free[bk] = stt(dst[:, :], PS[bk][:, :], 1.0 if what == "k" else 128.0 ** -0.5, SG[:, :],
                                       ALU.mult, ALU.mult, w=(m, done, factor))
                elif what == "g":
                    t = free[bk] = tt(G[x % 2][:, :], PS[bk][:, :], SG[:, :], ALU.mult,
                                      w=(m, tok.get(("gfree", x % 2)), factor))
                    tok[("g", n)] = t
                else:
                    tv = free[bk] = tt(VR[:, :], PS[bk][:, :], SG[:, :], ALU.mult, w=(m, tok.get("vr"), factor))

                    def rest():
                        m2 = tok["vr"] = turn4(7, [VR[:, 128 * q:128 * q + 128] for q in range(4)], (tv,))
                        tok[("v", n)] = free[7] = act(W[i][:, :], PS[7][:, :], w=(m2, done))
                    defer.append(rest)
                    t = None
                tok.setdefault(n, []).append(t)

            def products(n):
                i = n % 3
                for x in range(4):
                    b_, c0 = SBK[x]
                    m = mms([(PS[b_][:, c0:c0 + WID[x]], K[i][:, 128 * x:128 * x + 128],
                              Q[i][:, 128 * x:512], c0 == 0, True)], w=(free[b_], tok[n]))
                    tok[("z", x)] = m
                return m

            def weighted(n, ready, bk):
                i = n % 3
                its = [(PS[bk][:, 128 * x:512], W[i][:, 128 * x:128 * x + 128], AA[:, OFF[x]:OFF[x] + WID[x]],
                        x == 0, x == 3, ready[x]) for x in range(4)]
                m = mms(its, w=(free[bk], tok[("v", n)]))
                tok["aa"] = tok[("used", n)] = m
                return m

            def r1(n):
                products(n)
                ready = []
                for y in range(4):
                    b_, c0 = SBK[y]
                    t = tt(AA[:, OFF[y]:OFF[y] + WID[y]], PS[b_][:, c0:c0 + WID[y]],
                           DEC[HEADS[n][1]][:, 0:WID[y]], ALU.mult, w=(tok[("z", 3)], rtok, tok.get("aa")))
                    free[b_] = t
                    ready.append(t)
                tok[("rd", n)] = ready

            def r2(n):
                m = weighted(n, tok[("rd", n)], 5)
                tok[("o", n)] = free[5] = act(OBS[1][:, :], PS[5][:, :], w=(m, tok.get("ob1")))

            def r3(n):
                OB, OC = OBS[1], OCS[1]
                m = mms([(PS[6][:, :], ONES, OB[:, :], True, True)], w=(tok[("o", n)], free[6]))
                t = free[6] = stt(OB[:, :], PS[6][:, :], -1.0 / 128, OB[:, :], ALU.mult, ALU.add,
                                  w=(m, tok[("o", n)]))
                tok[("q", n)] = act(OC[:, :], OB[:, :], ACT.Square, w=(t, tok.get("oc1")))

            def s1(n):
                products(n)
                parts, ts_ = [], []
                for y in range(4):
                    b_, c0 = SBK[y]
                    a_ = AA[:, OFF[y]:OFF[y] + WID[y]]
                    ts_.append(act(a_, PS[b_][:, c0:c0 + WID[y]], ACT.Abs, w=(tok[("z", 3)], tok.get("aa"))))
                zt = ts_[3]
                for y in range(4):
                    b_, c0 = SBK[y]
                    z = PS[b_][:, c0:c0 + WID[y]]
                    a_ = AA[:, OFF[y]:OFF[y] + WID[y]]
                    s_ = SPL[:, OFF[y]:OFF[y] + WID[y]]
                    t = act(a_, a_, ACT.Exp, scale=-1.0, w=(ts_[y],))
                    t = act(a_, a_, ACT.Ln, bias=ONE, w=(t, kontok))
                    t = stt(s_, z, 0.0, a_, ALU.max, ALU.add, w=(t, zt, tok.get("sp")))
                    t = free[b_] = tt(a_, z, s_, ALU.subtract, w=(t,))
                    t = tt(s_[:, 0:128], s_[:, 0:128], STRICT, ALU.mult, w=(t,))
                    parts.append(t)
                tok[("parts", n)] = parts

            def s2(n):
                parts = tok[("parts", n)]
                ready = []
                ms = []
                for y in (3, 2, 1, 0):
                    b_, c0 = LBK[y]
                    its = []
                    for j in range(y, 4):
                        its.append((PS[b_][:, c0 + 128 * (j - y):c0 + WID[y]], UNEG if j == y else NONES,
                                    SPL[:, OFF[j]:OFF[j] + WID[j]], j == y and y != 1, j == 3, parts[j]))
                    ms.append(mms(its, w=(free[b_],)))
                tok["sp"] = ms[3]
                ms = ms[::-1]
                for y in (3, 2, 1, 0):
                    b_, c0 = LBK[y]
                    a_ = AA[:, OFF[y]:OFF[y] + WID[y]]
                    t = free[b_] = tt(a_, a_, PS[b_][:, c0:c0 + WID[y]], ALU.add,
                                      w=(ms[1] if y == 3 else ms[y], parts[y]))
                    t = act(a_, a_, ACT.Exp, w=(t,))
                    ready.append(tt(a_[:, 0:128], a_[:, 0:128], STRICT, ALU.mult, w=(t,)))
                tok[("rd", n)] = ready[::-1]

            def s3(n):
                m = weighted(n, tok[("rd", n)], 2)
                tok[("o", n)] = t = free[2] = act(OBS[0][:, :], PS[2][:, :], w=(m, tok.get("ob0")))
                tok[("q", n)] = act(OCS[0][:, :], OBS[0][:, :], ACT.Square, w=(t, tok.get("oc0")))

            def finish(n):
                kind, x = HEADS[n]
                k = x if kind == "r" else 4 + x
                i = 1 if kind == "r" else 0
                OB, OC, bk = OBS[i], OCS[i], 6 if kind == "r" else 7
                m = mms([(PS[bk][:, :], ONES, OC[:, :], True, True)], w=(tok[("q", n)], free[bk]))
                q1 = free[bk] = act(OC[:, :], PS[bk][:, :], ACT.Ln, bias=EPSC, scale=1.0 / 128, w=(m,))
                q2 = act(OC[:, :], OC[:, :], ACT.Exp, scale=-0.5, w=(q1,))
                gc = col("ret_norm_g_2" if kind == "r" else "sb_norm_g_2", 4 * l + x)
                y1 = stt(OB[:, :], OB[:, :], gc, OC[:, :], ALU.mult, ALU.mult, w=(q2, tok[("o", n)], tok[("q", n)]))
                tok[f"oc{i}"] = y1
                if kind == "r":
                    y1 = tt(OB[:, :], OB[:, :], G[x % 2][:, :], ALU.mult, w=(y1, tok[("gs", n)]))
                    tok[("gfree", x % 2)] = y1
                y2 = act(chunk(H2H, k), OB[:, :], w=(y1,))
                y3 = tt(chunk(H2L, k), OB[:, :], chunk(H2H, k).bitcast(F32), ALU.subtract, w=(y2,))
                tok[f"ob{i}"] = mixed[k] = y3

            def gate_silu(n):
                table("silu")
                g = G[HEADS[n][1] % 2]
                tok[("gs", n)] = act(g[:, :], g[:, :], ACT.Silu, w=(tok[("g", n)],))
                table("natural_log_exp")

            events = []
            for x in range(4):
                a, b = 7 * x + 3, 7 * x + 7
                events += [(a + 0.5, 2 * x, s1), (a + 2.5, 2 * x, s2), (a + 3.8, 2 * x, s3), (a + 5, 2 * x, finish),
                           (b + 0.5, 2 * x + 1, r1), (b + 0.6, 2 * x + 1, gate_silu), (b + 1.5, 2 * x + 1, r2),
                           (b + 2.3, 2 * x + 1, r3), (b + 3.2, 2 * x + 1, finish)]
            events.sort(key=lambda e: (e[0], e[1]))

            def run_ev(until, events=events):
                while events and events[0][0] <= until:
                    _, n, fn = events.pop(0)
                    fn(n)

            for t_ in range(28):
                run_ev(t_)
                proj(t_)
                if t_ == 0:
                    t1 = tt(COS, COS, SG[:, :], ALU.mult, w=(rtok, factor))
                    turned = tt(SIN, SIN, SG[:, :], ALU.mult, w=(t1,))
                if l == 0 and 1 <= t_ <= 8:
                    ssa[0] = stt(xk(t_ - 1), xk(t_ - 1), col("final_g", t_ - 1), SS[:, :], ALU.mult, ALU.mult,
                                 w=(hx,))
            while defer:
                defer.pop(0)()
            run_ev(28.6)
            hfree = PE.last()
            order_ = (4, 0, 5, 1, 6, 2, 7, 3)
            hooks = {5: lambda: run_ev(29.9), 11: lambda: run_ev(30.5), 17: lambda: run_ev(1000)}
            group(["w_out_2"] * 3, [H2] * 3, [mixed] * 3, korder=order_, split=7, hooks=hooks.items(),
                  banks=(0, 1, 3))
            hx = []
            for n in range(8):
                bk, m = tile("w_out_2", H2, mixed)
                t = residual(n, nb, m, bk)
                hx.append(split_x(n, cols("norm2_g_2", 8 * l, 8), (t, hfree)))
            prepare(cur[0] + 2)
            factor = norm_r(nb, SG[:, :], (DVE.last(), PO.last()))
            table("silu")
            barrier()
            lay.close()
            lay = ExitStack()
            nb = norm_bufs(lay, f"e{l}")
            hx = ffn(f"d{l}", nb, lay, ("w_gate_2", "w_up_2", "w_down_2"), hx, None, None, factor=factor,
                     gain=None if l else cols("norm1_g_2", 8, 8))
            prepare(cur[0] + 2)
            factor = r = norm_r(nb, SG[:, :], (DVE.last(), PO.last()))
            if l:
                for k in range(8):
                    t = stt(xk(k), xk(k), col("final_g_2", k), SG[:, :], ALU.mult, ALU.mult, w=(r,))
                    SP.wait(t)
                    otk = s_out.sig(nc.sync.dma_start(out[128 * k:128 * k + 128, :], xk(k)))
            barrier()
            lay.close()
        SP.wait(otk, PE.last(), DVE.last(), SC.last(), PO.last())


def lay_out(inputs):
    parts = []
    for unit, _, tiles in plan():
        block = []
        for name, layer, k0, kn, n, nn in tiles:
            m = inputs[name] if layer is None else inputs[name][layer]
            if name == "pool_w_grp":
                m = m.reshape(1024, 256)
            b = m[128 * k0:128 * (k0 + kn), 128 * n:128 * (n + nn)]
            if unit == "ada":
                block.append(b.T)
            else:
                block.append(b.reshape(kn, 128, nn * 128).transpose(1, 0, 2).reshape(128, -1))
        parts.append(np.concatenate(block, axis=1).reshape(-1))
    stream = np.concatenate(parts)
    cols = np.concatenate([np.ascontiguousarray(inputs[n]).reshape(-1, 128).T for n, _ in COLS], axis=1)
    assert cols.shape == (128, NCOL)
    return stream, np.ascontiguousarray(inputs["c"][0]), np.ascontiguousarray(cols), np.ascontiguousarray(inputs["x"][0].T)


def kernel(**inputs):
    import concourse.bacc as _bacc
    from concourse.bass_utils import run_bass_kernel_spmd as _run

    ins = {k: np.asarray(v) for k, v in inputs.items()}
    stream, c, cols, xt = lay_out(ins)
    base, att, ret = tables()
    arrays = {"stream": stream, "c": c, "cols": cols, "xt": xt, "base": base, "att": att, "ret": ret}
    nc = _bacc.Bacc("TRN2", target_bir_lowering=False, num_devices=1, dynamic_dma_scratch_size=1024)
    args = [nc.dram_tensor(n, a.shape, F32, kind="ExternalInput").ap() for n, a in arrays.items()]
    y = nc.dram_tensor("y", (D, S), F32, kind="ExternalOutput").ap()
    program(nc, *args, y)
    r = _run(nc, [arrays], core_ids=[0])
    return np.ascontiguousarray(r.results[0]["y"].T).reshape(1, S, D)
```

```python
import math
from contextlib import ExitStack

import numpy as np
import concourse.bass as bass
from concourse import mybir

F32 = mybir.dt.float32
F32R = mybir.dt.float32r
ALU = mybir.AluOpType
ACT = mybir.ActivationFunctionType
AX_X = mybir.AxisListType.X

D, S, F, KC, FC, HC = 1024, 512, 2816, 8, 22, 11
NEG = -1.0e30
EPS = 1e-6
SLOT = 2048
WSLOT = HC * 128
GRP = 5

PAIR_TILES = [("w_kv", 0, "k"), ("attn_w_q", 0, "q"), ("w_kv", 1, "k"), ("attn_w_q", 1, "q"), ("w_kv", 2, "k"),
              ("attn_w_q", 2, "q"), ("w_kv", 0, "v"), ("w_kv", 1, "v"), ("w_kv", 2, "v")]
HEADS = [(kind, x) for x in range(4) for kind in "sr"]
HEAD_TILES = {"r": (("k", 4), ("q", 0), ("v", 8), ("g", 12)), "s": (("k", 20), ("q", 16), ("v", 24))}



def plan():
    def ada(name, layer, first, blocks):
        return [("ada", first + i, [(name, layer, 0, KC, b, 1) for b in blocks[i:i + 2]])
                for i in range(0, len(blocks), 2)]

    def pairs(tiles):
        return [("main", None, tiles[i:i + 2]) for i in range(0, len(tiles), 2)]

    def mix(main, side, n=1):
        out, side = [], list(side)
        for m in main:
            out.append(m)
            out += side[:n]
            side = side[n:]
        return out, side

    def square(name, layer, blocks):
        return [(name, layer, 0, KC, n, 1) for n in blocks]

    def ffn(gate, up, down, layer):
        out = []
        for half in range(2):
            for j in range(half * HC, half * HC + HC):
                out.append(("main", None, [(gate[0], layer, 0, KC, gate[1] + j, 1),
                                           (up[0], layer, 0, KC, up[1] + j, 1)]))
            out += [("main", None, [(down, layer, half * HC, HC, n, 1)]) for n in range(8)]
        return out

    units = []
    shift, scale = ada("ada_w", 0, 0, list(range(8))), ada("ada_w", 0, 8, list(range(8, 16)))
    for i in range(4):
        units += [shift[i], scale[i], ("main", None, [("pool_w_in", 0, 2 * i, 2, 8 - GRP, GRP)])]
    side = ada("ada_w", 0, 16, list(range(16, 48)))
    pool = pairs(square("pool_w_in", 0, range(8 - GRP)) + square("pool_w_grp", 0, range(2))
                 + square("pool_w_out", 0, range(8)))
    units += pool[:1]
    out, side = mix(pool[1:], side, 2)
    units += out
    side = side + ada("ada_w", 1, 48, list(range(48))) + ada("kv_ada_w", None, 96, list(range(16)))
    out, side = mix(ffn(("ffn_w_up", 0), ("ffn_w_up", FC), "ffn_w_down", 0), side)
    assert not side
    units += out
    qkv = []
    for p in range(8):
        for name, g, what in PAIR_TILES:
            qkv.append((name, 0 if what == "q" else None, 0, KC, (24 if what == "v" else 0) + 8 * g + p, 1))
    units += pairs(qkv)
    units += pairs(square("attn_w_o", 0, range(8)))
    units += ffn(("ffn_w_up", 0), ("ffn_w_up", FC), "ffn_w_down", 1)
    for l in range(2):
        w = []
        for kind, x in HEADS:
            w += square("w_in_2", l, [b + x for _, b in HEAD_TILES[kind]])
        units += pairs(w)
        units += pairs(square("w_out_2", l, range(8)))
        units += ffn(("w_gate_2", 0), ("w_up_2", 0), "w_down_2", l)
    return units


def words(tile):
    return tile[3] * tile[5] * 128


COLS = [("ada_b", 96), ("kv_ada_b", 16), ("norm1_g", 16), ("norm2_g", 16), ("pool_scale", 8),
        ("kv_norm_g", 8), ("final_g", 8), ("norm1_g_2", 16), ("norm2_g_2", 16), ("final_g_2", 8),
        ("ret_norm_g_2", 8), ("sb_norm_g_2", 8), ("ffn_conv_w", 132), ("ffn_conv_b", 44)]
COL = {}
NCOL = 0
for _n, _k in COLS:
    COL[_n] = NCOL
    NCOL += _k


def slopes():
    def pow2(m):
        start = 2.0 ** (-(2.0 ** -(math.log2(m) - 3)))
        return [start ** (i + 1) for i in range(m)]
    s = np.asarray(pow2(32) + pow2(64)[0::2][:16], dtype=np.float32)
    return (-np.sort(-s)).reshape(3, 16)


def tables():
    p = np.arange(128)[:, None]
    q = np.arange(128)[None, :]
    base = np.zeros((128, 576), np.float32)
    base[:, 0:128] = p == q
    base[:, 128:256] = -(p > q).astype(np.float32)
    base[:, 256:384] = -1.0
    base[:, 384:512] = p < q
    for g, w in enumerate((2, 4, 8, 16)):
        base[:, 512 + 16 * g:528 + 16 * g] = 1.0 / np.minimum(np.arange(16) + 1, w).astype(np.float32)[None, :]
    att = np.zeros((128, 1152), np.float32)
    for n in range(7):
        delta = 4 * (p - q) + (3 - n)
        att[:, 128 * n:128 * n + 128] = np.where((delta >= 0) & (delta <= 128), -delta, NEG)
    att[:, 896:1024] = np.where(p >= q, -4 * (p - q), NEG)
    att[:, 1024:1152] = np.where((p >= q) & ((p - q) % 4 == 0), -4 * (p - q), NEG)
    ret = np.zeros((128, 3072), np.float32)
    t = np.arange(512)[None, :]
    for h in range(4):
        lg = np.log1p(-np.exp2(-5.0 - h))
        w = np.exp(lg * np.abs(t - p)) * 128.0 ** -0.5
        ret[:, 512 * h:512 * h + 512] = np.where(t // 64 >= p // 64, w, 0.0)
    inv = (1.0 / (np.float32(10000.0) ** (np.arange(0, 128, 2, dtype=np.float32) / np.float32(128)))).astype(np.float32)
    ang = (np.arange(512, dtype=np.float32)[None, :] * inv[:, None]).astype(np.float32)
    ret[:, 2048:2560] = np.concatenate([np.cos(ang), np.cos(ang)])
    ret[:, 2560:3072] = np.concatenate([-np.sin(ang), np.sin(ang)])
    return base, att, ret


class Engine:

    def __init__(self, ns, sem):
        self.ns, self.sem, self.n, self.met = ns, sem, 0, {}

    def wait(self, *tokens):
        for t in tokens:
            if t is None:
                continue
            if isinstance(t, list):
                self.wait(*t)
                continue
            sem, value = t
            if self.met.get(id(sem), 0) < value:
                self.ns.wait_ge(sem, value)
                self.met[id(sem)] = value

    def sig(self, ins):
        ins.then_inc(self.sem, 1)
        self.n += 1
        return (self.sem, self.n)

    def last(self):
        return (self.sem, self.n)


class Slot:

    def __init__(self, sem):
        self.sem, self.n = sem, 0

    def sig(self, ins):
        ins.then_inc(self.sem, 16)
        self.n += 16
        return (self.sem, self.n)


def program(nc, stream, cd, colsd, xt, basd, attd, retd, out):
    units = plan()
    usize = [sum(words(t) for t in u[2]) for u in units]
    offs = np.concatenate([[0], np.cumsum([128 * n for n in usize])])
    tiles = [(u, j) for u, unit in enumerate(units) if unit[0] == "main" for j in range(len(unit[2]))]
    SL = slopes()
    top = ExitStack()
    with top:
        def sbuf(name, n, dt=F32, ctx=top):
            return ctx.enter_context(nc.sbuf_tensor(name, [128, n], dt))

        def sem(name):
            return top.enter_context(nc.semaphore(name))

        XT = sbuf("XT", 4096)
        H1H, H1L = sbuf("H1H", 4096, F32R), sbuf("H1L", 4096, F32R)
        RAW = [sbuf(f"RAW{i}", SLOT) for i in range(2)]
        WH = [sbuf(f"WH{i}", WSLOT, F32R) for i in range(3)]
        WL = [sbuf(f"WL{i}", WSLOT, F32R) for i in range(3)]
        SS, SG = sbuf("SS", 512), sbuf("SG", 512)
        CO = sbuf("CO", NCOL)
        MOD = sbuf("MOD", 112)
        AB = sbuf("AB", 40)
        KON = sbuf("KON", 2)
        BAS = sbuf("BAS", 576)
        ONES = sbuf("ONES", 128)[:, :]
        PS = [top.enter_context(nc.psum_tensor(f"PS{i}", [128, 512], F32)) for i in range(8)]
        free = [None] * 8

        PE, DVE = Engine(nc.tensor, sem("pe")), Engine(nc.vector, sem("dve"))
        SC, PO = Engine(nc.scalar, sem("act")), Engine(nc.gpsimd, sem("pool"))
        SP = Engine(nc.sync, None)
        raw = [Slot(sem(f"raw{i}")) for i in range(2)]
        ara = [Slot(sem(f"ara{i}")) for i in range(3)]
        s_c, s_co, s_bas, s_att, s_ret = (Slot(sem(n)) for n in ("d_c", "d_co", "d_bas", "d_att", "d_ret"))
        s_x = [Slot(sem(f"d_x{i}")) for i in range(2)]
        s_out = Slot(sem("d_out"))

        IDENT, STRICT = BAS[:, 0:128], BAS[:, 384:512]
        MEANS = BAS[:, 512:576]
        ONE, EPSC = KON[:, 0:1], KON[:, 1:2]
        top.enter_context(nc.Block())

        def chunk(buf, k):
            return buf[:, 512 * k:512 * k + 512]

        def xk(k):
            return chunk(XT, k)

        def cols(name, i, n):
            return CO[:, COL[name] + i:COL[name] + i + n]

        def col(name, i):
            return cols(name, i, 1)

        def act(out_, in_, fn=ACT.Copy, w=(), **kw):
            SC.wait(*w)
            return SC.sig(nc.scalar.activation(out_, in_, fn, **kw))

        def tt(out_, a, b, op, w=(), e=None):
            e = e or DVE
            e.wait(*w)
            return e.sig(e.ns.tensor_tensor(out_, a, b, op))

        def stt(out_, a, s, b, op0, op1, w=()):
            DVE.wait(*w)
            return DVE.sig(nc.vector.scalar_tensor_tensor(out_, a, s, b, op0, op1))

        def ts(out_, a, s1, s2, op0, op1=None, w=()):
            DVE.wait(*w)
            if op1 is None:
                return DVE.sig(nc.vector.tensor_scalar(out_, a, s1, None, op0))
            return DVE.sig(nc.vector.tensor_scalar(out_, a, s1, s2, op0, op1))

        def mms(items, w=()):
            PE.wait(*w)
            for it in items:
                if len(it) > 5:
                    PE.wait(it[5])
                ins = nc.tensor.matmul(it[0], it[1], it[2], start=it[3], stop=it[4], skip_group_check=True)
            return PE.sig(ins)

        def turn4(bk, srcs, w):
            PE.wait(*w, free[bk], bastok)
            for n, src in enumerate(srcs):
                ins = nc.tensor.transpose(PS[bk][:, 128 * n:128 * n + 128], src, IDENT)
            return PE.sig(ins)

        def table(name):
            nc.scalar.preload_act_table_set(name + "_and_others")

        nload = [0]
        order = {"main": 0, "ada": 0}
        place, loaded, ready_at = {}, {}, {}
        rawfree, arafree = [None, None], [None] * 3
        nunit, ntile = [0], [0]
        wfree = [None] * 3
        wtok = {}
        usepool = [False]
        ahead = [0]
        AR, condtok, modtok = [], [None], [None]

        def load():
            while nload[0] < len(units):
                u = nload[0]
                kind = units[u][0]
                n = order[kind]
                ring = 2 if kind == "main" else 3
                if n >= ring and not ready_at.get((kind, n - ring)):
                    return
                i = n % ring
                place[u] = i
                SP.wait((rawfree if kind == "main" else arafree)[i])
                src = stream[int(offs[u]):int(offs[u + 1])].rearrange("(p n) -> p n", p=128)
                dst = (RAW if kind == "main" else AR)[i]
                slot = (raw if kind == "main" else ara)[i]
                loaded[u] = slot.sig(nc.sync.dma_start(dst[:, 0:usize[u]], src))
                order[kind] += 1
                nload[0] += 1

        seen = {"main": 0, "ada": 0}

        def finished(kind):
            ready_at[(kind, seen[kind])] = True
            seen[kind] += 1
            load()

        def ada_unit(u):
            i = place[u]
            first = units[u][1]
            for q in range(2):
                src = AR[i][:, 1024 * q:1024 * q + 1024]
                bias = col("ada_b", first + q) if first < 96 else col("kv_ada_b", first - 96 + q)
                DVE.wait(loaded[u], condtok[0], cotok)
                t = DVE.sig(nc.vector.tensor_tensor_reduce(src, src, COND[:, :], 1.0, bias, ALU.mult, ALU.add,
                                                           MOD[:, first + q:first + q + 1]))
            arafree[i] = modtok[0] = t
            finished("ada")

        def prepare(t):
            while ntile[0] <= t and ntile[0] < len(tiles):
                u, j = tiles[ntile[0]]
                while nunit[0] < u:
                    if units[nunit[0]][0] == "ada":
                        ada_unit(nunit[0])
                    nunit[0] += 1
                spec = units[u][2][j]
                base = sum(words(x) for x in units[u][2][:j])
                n, i, s = words(spec), place[u], ntile[0] % 3
                src = RAW[i][:, base:base + n]
                hi = act(WH[s][:, 0:n], src, w=(loaded[u], wfree[s]))
                e = PO if usepool[0] else DVE
                lo = tt(WL[s][:, 0:n], src, WH[s][:, 0:n].bitcast(F32), ALU.subtract, w=(hi, loaded[u], wfree[s]),
                        e=e)
                wtok[ntile[0]] = lo
                if j == len(units[u][2]) - 1:
                    rawfree[i] = lo
                    nunit[0] = u + 1
                    finished("main")
                ntile[0] += 1

        cur = [0]

        def take(name):
            t = cur[0]
            cur[0] += 1
            u, j = tiles[t]
            assert units[u][2][j][0] == name, (name, units[u][2][j])
            prepare(t)
            prepare(t + ahead[0])
            return t % 3, wtok[t], units[u][2][j]

        ring = [0]
        ALLB = (0, 1, 2, 3, 4, 5, 6)

        def bank(banks=ALLB):
            ring[0] += 1
            return banks[ring[0] % len(banks)]

        def three(bank_ap, s, o, hi, lo, first, last, rt=None):
            wh, wl = WH[s][:, o:o + 128], WL[s][:, o:o + 128]
            return [(bank_ap, wh, hi, first, False, rt), (bank_ap, wh, lo, False, False),
                    (bank_ap, wl, hi, False, last)]

        early_tiles = []

        def tile(name, hl, ready=None, banks=ALLB, middle=None):
            if early_tiles:
                t, bk, m = early_tiles.pop(0)
                prepare(t + ahead[0])
                for k in (2, 4) if middle else ():
                    middle(k)
                return bk, m
            s, tok, spec = take(name)
            bk = bank(banks)
            hi, lo = hl
            items = []
            for k in range(spec[3]):
                if k in (2, 4) and middle:
                    mms(items, w=(tok, free[bk]))
                    items = []
                    middle(k)
                items += three(PS[bk][:, :], s, 128 * k, chunk(hi, k), chunk(lo, k), k == 0, k == spec[3] - 1,
                               ready[k] if ready else None)
            m = mms(items, w=(tok, free[bk]))
            wfree[s] = m
            return bk, m

        def group(names, hls, readys, korder=tuple(range(8)), split=4, hooks=(), banks=ALLB):
            t0 = cur[0]
            hooks = dict(hooks)
            prepare(t0 + len(names) - 1)
            got = []
            for n in names:
                t = cur[0]
                cur[0] += 1
                u, j = tiles[t]
                assert units[u][2][j][0] == n
                got.append((t, bank(banks)))
            toks = []

            def part(x, ks):
                t, bk = got[x]
                items = []
                for k in ks:
                    items += three(PS[bk][:, :], t % 3, 128 * k, chunk(hls[x][0], k), chunk(hls[x][1], k),
                                   k == korder[0], k == korder[-1], readys[x][k] if readys[x] else None)
                return mms(items, w=(wtok[t], free[bk]))

            for n, k in enumerate(korder[:split]):
                for x in range(len(names)):
                    part(x, [k])
                    if 3 * n + x in hooks:
                        hooks[3 * n + x]()
            for x in range(len(names)):
                m = part(x, korder[split:])
                wfree[got[x][0] % 3] = m
                early_tiles.append((got[x][0], got[x][1], m))
                prepare(t0 + 3 + x)

        def barrier(*others):
            toks = [e.last() for e in (PE, DVE, SC, PO) if e.n]
            for e in (DVE, SC, PO, *others):
                e.wait(*toks)

        ssa, sga = [None], [None]
        sq7 = [None]

        def norm_bufs(ctx, tag, squares=False, more=False):
            b = {}
            if not more:
                b.update(SQ=[sbuf(f"SQ{i}{tag}", 512, F32, ctx) for i in range(2)], sq=[None, None], n=0)
            if not squares:
                b.update(R=sbuf(f"R{tag}", 512, F32, ctx), T=[sbuf(f"T{i}{tag}", 512, F32, ctx) for i in range(3)],
                         V=[sbuf(f"V{i}{tag}", 512, F32, ctx) for i in range(4)], tf=[None] * 3, vf=[None] * 4)
            return b

        def add_square(b, k, w, acc=None, state=None, scale=1.0):
            acc, state = acc or SS, state or ssa
            if k == 0:
                state[0] = act(acc[:, :], xk(0), ACT.Square, scale=scale, w=(w, state[0]))
                return
            i = b["n"] % 2 if k < 7 or acc is SG else 1
            b["n"] = i + 1
            t = act(b["SQ"][i][:, :], xk(k), ACT.Square, scale=scale, w=(w, b["sq"][i]))
            if k == 7 and acc is SS:
                sq7[0] = b["sq"][1] = t
                return
            state[0] = b["sq"][i] = tt(acc[:, :], acc[:, :], b["SQ"][i][:, :], ALU.add, w=(t, state[0]))

        def rsqrt_of(bk, out_, scale, w):
            t = free[bk] = act(out_, PS[bk][:, :], ACT.Ln, bias=EPSC, scale=scale, w=(*w, kontok))
            return act(out_, out_, ACT.Exp, scale=-0.5, w=(t,))

        def norm_r(b, out_=None, w=(), i=None):
            i = bank() if i is None else i
            mms([(PS[i][:, :], ONES, SS[:, :], True, False)], w=(ssa[0], free[i], kontok))
            m = mms([(PS[i][:, :], ONES, b["SQ"][1][:, :], False, True)], w=(sq7[0],))
            ssa[0] = b["sq"][1] = m
            return rsqrt_of(i, out_ or b["R"][:, :], 1.0 / D, (m, *w))

        def norm_apply(b, r, outs, w=(), ks=tuple(range(8))):
            toks = []

            def buf(k, n):
                return (k * len(outs) + n) % 4

            def scale(k):
                i = k % 3
                t = tt(b["T"][i][:, :], xk(k), b["R"][:, :], ALU.mult, w=(r, *w, b["tf"][i]))
                got = [t]
                for n, (_, _, gain, shift, _) in enumerate(outs):
                    if n or len(outs) == 1:
                        j = buf(k, n)
                        got.append(ts(b["V"][j][:, :], b["T"][i][:, :], gain[:, k:k + 1], shift[:, k:k + 1],
                                      ALU.mult, ALU.add, w=(t, b["vf"][j])))
                return got

            def affine(out_, k, n, t):
                return act(out_, b["T"][k % 3][:, :], ACT.Identity, scale=outs[n][2][:, k:k + 1],
                           bias=outs[n][3][:, k:k + 1], w=(t, *w))

            got = scale(ks[0])
            for k in ks:
                more = k != ks[-1]
                his = {n: affine(outs[n][4](chunk(outs[n][0], k)), k, n, got[0]) for n in reversed(range(len(outs)))}
                if len(outs) > 1:
                    SC.wait(b["vf"][buf(k, 0)])
                    v0 = affine(b["V"][buf(k, 0)][:, :], k, 0, got[0])
                    got = [got[0], v0, *got[1:]]
                b["tf"][k % 3] = [*got[1:], *his.values(), SC.last()]
                nxt = scale(k + 1) if more else None
                row = []
                for n, (hi, lo, _, _, view) in enumerate(outs):
                    j = buf(k, n)
                    pool = (n == 0) if len(outs) > 1 else (k % 2 == 1)
                    l = b["vf"][j] = tt(view(chunk(lo, k)), b["V"][j][:, :], view(chunk(hi, k)).bitcast(F32),
                                        ALU.subtract, w=(got[n + 1], his[n]), e=PO if pool else DVE)
                    row.append(l)
                toks.append(row)
                got = nxt
            return [[g[n] for g in toks] for n in range(len(outs))]

        def plain(ap):
            return ap

        def permuted(ap):
            return ap.rearrange("p (r j) -> p j r", r=4)

        def mod(first, n=8):
            return MOD[:, first:first + n]

        def split_x(k, gain, w):
            h = act(chunk(H1H, k), xk(k), scale=gain[:, k:k + 1], w=w)
            return stt(chunk(H1L, k), xk(k), gain[:, k:k + 1], chunk(H1H, k).bitcast(F32), ALU.mult, ALU.subtract,
                       w=(h, *w))

        def gains(at, name, i, scale_col, n=8):
            return stt(AB[:, at:at + n], mod(scale_col, n), 1.0, cols(name, i, n), ALU.add, ALU.mult,
                       w=(modtok[0], cotok))

        factor, late = [None], []

        def later(k):
            while late and k == 2:
                late.pop(0)()

        def residual(n, b, m, bk, gcol=None, square=True, second=False):
            if gcol is None:
                t = tt(xk(n), PS[bk][:, :], xk(n), ALU.add, w=(m,))
            else:
                t = stt(xk(n), PS[bk][:, :], gcol, xk(n), ALU.mult, ALU.add, w=(m,))
            free[bk] = t
            if square:
                add_square(b, n, t)
                if second:
                    add_square(b, n, t, SG, sga, col("final_g", n))
            return t

        def split_out(bk, hi, lo, m, scale, w=()):
            h = act(hi, PS[bk][:, :], scale=scale, w=(m, *w))
            l = stt(lo, PS[bk][:, :], scale, hi.bitcast(F32), ALU.mult, ALU.subtract, w=(h,))
            free[bk] = l
            return l

        H1 = (H1H, H1L)

        early = ExitStack()
        AR += [sbuf(f"AR{i}", SLOT, F32, early) for i in range(3)]
        COND = sbuf("COND", 1024, F32, early)
        nb = norm_bufs(early, "a")
        table("silu")
        ctok = s_c.sig(nc.scalar.dma_start(COND[:, :], cd.partition_broadcast(128)))
        cotok = s_co.sig(nc.sync.dma_start(CO[:, :], colsd))
        xtok = []
        for q in range(2):
            xtok += [s_x[q].sig(nc.sync.dma_start(XT[:, 2048 * q:2048 * q + 2048].rearrange("p (k t) -> p k t", k=4),
                                                  xt[512 * q:512 * q + 512, :].rearrange("(k p) t -> p k t", p=128)))]
        load()
        bastok = s_bas.sig(nc.sync.dma_start(BAS[:, :], basd))
        PO.sig(nc.gpsimd.memset(ONE, 1.0))
        PO.sig(nc.gpsimd.memset(ONES[:, :], 1.0))
        kontok = PO.sig(nc.gpsimd.memset(EPSC, EPS))
        condtok[0] = act(COND[:, :], COND[:, :], ACT.Silu, w=(ctok,))
        table("natural_log_exp")
        for k in range(8):
            add_square(nb, k, xtok[k // 4])
        r = norm_r(nb)
        usepool[0] = True
        h1 = []
        kb = [0, 1, 2, 3, 4]
        for i in range(4):
            s, tok, spec = take("pool_w_in")
            ta = gains(2 * i, "norm1_g", 2 * i, 8 + 2 * i, 2)
            h1 += norm_apply(nb, r, [(H1H, H1L, AB[:, 0:8], mod(0), plain)], w=(ta,), ks=(2 * i, 2 * i + 1))[0]
            for j in range(2):
                for x in range(GRP):
                    k = 2 * i + j
                    m = mms(three(PS[kb[x]][:, :], s, 128 * (GRP * j + x), chunk(H1H, k), chunk(H1L, k),
                                  k == 0, k == 7, h1[k]), w=(tok, free[kb[x]]))
            wfree[s] = m
            if i < 3:
                prepare(cur[0])
        ahead[0] = 2
        prepare(cur[0] + 1)

        pool = ExitStack()
        H2H, H2L = sbuf("H2Ha", 4096, F32R, pool), sbuf("H2La", 4096, F32R, pool)
        U = [sbuf(f"U{i}", 528, F32, pool) for i in range(2)]
        V = [[sbuf(f"V{i}{j}", 528, F32, pool) for i in range(2)] for j in range(2)]
        tz = None
        for t_ in (*U, *V[0], *V[1]):
            tz = DVE.sig(nc.vector.memset(t_[:, 0:16], 0.0))
        ufree, vfree, h2 = [None, None], [None, None], [None] * 8

        pend, pcount = [], [0]

        def pooled(n, bk, m):
            g, i = n // 2, pcount[0] % 2
            pcount[0] += 1
            u = U[i]
            t = free[bk] = act(u[:, 16:528], PS[bk][:, :], w=(m, ufree[i], tz))
            src, sh, dst = u, 1, 0
            DVE.wait(vfree[i])
            for _ in range(g + 1):
                d = V[i][dst]
                t = tt(d[:, 16:528], src[:, 16:528], src[:, 16 - sh:528 - sh], ALU.add, w=(t, tz))
                src, sh, dst = d, sh * 2, 1 - dst
            p = V[i][dst]
            t1 = stt(p[:, 16:528], src[:, 16:528], 1.0 / sh, u[:, 16:528], ALU.mult, ALU.subtract, w=(t,))
            t2 = tt(p[:, 16:16 + sh], src[:, 16:16 + sh], MEANS[:, 16 * g:16 * g + sh], ALU.mult,
                    w=(t1, bastok))
            t3 = tt(p[:, 16:16 + sh], p[:, 16:16 + sh], u[:, 16:16 + sh], ALU.subtract, w=(t2,))
            ufree[i] = t3
            pend.append((n, i, p, t3))

        def pooled_split():
            n, i, p, t3 = pend.pop(0)
            hh = act(chunk(H2H, n), p[:, 16:528], w=(t3,))
            h2[n] = vfree[i] = tt(chunk(H2L, n), p[:, 16:528], chunk(H2H, n).bitcast(F32), ALU.subtract,
                                  w=(t3, hh), e=PO)

        pooled(3, kb[0], m)
        pooled(4, kb[1], m)
        pooled_split()
        for n in range(8 - GRP):
            bk, mt = tile("pool_w_in", H1, h1, banks=(5, 6, 7))
            for _ in range(2):
                x = pcount[0]
                if x < GRP:
                    pooled(8 - GRP + x, kb[x], m)
                    pooled_split()
            if n:
                pooled(*before)
                pooled_split()
            before = (n, bk, mt)
        pooled(*before)
        while pend:
            pooled_split()
        gfree = PE.last()
        h1 = [None] * 8
        for d in range(2):
            s, tok, _ = take("pool_w_grp")
            for g in (2, 3, 0, 1):
                bk = bank()
                items = []
                for i in range(2):
                    c = 2 * g + i
                    items += three(PS[bk][:, :], s, 128 * c, chunk(H2H, c), chunk(H2L, c), i == 0, i == 1, h2[c])
                m = mms(items, w=(tok, free[bk]))
                n = 2 * g + d
                h1[n] = split_out(bk, chunk(H1H, n), chunk(H1L, n), m, col("pool_scale", n), w=(gfree,))
            wfree[s] = m
        for n in range(8):
            bk, m = tile("pool_w_out", H1, h1)
            residual(n, nb, m, bk, MOD[:, 16 + n:17 + n])
        pool.close()
        barrier()

        gained = {}

        def ffn(tag, b, ctx, names, h, conv, gate, second=False, scaled=True, gain=None,
                last=False):
            GH, GL = sbuf(f"GH{tag}", HC * 512, F32R, ctx), sbuf(f"GL{tag}", HC * 512, F32R, ctx)
            Y = [sbuf(f"Y{tag}{i}", 512, F32, ctx) for i in range(2)]
            SI = [sbuf(f"SI{tag}{i}", 512, F32, ctx) for i in range(2)]
            gfree = None
            gt = [None, None]
            na, nv, nd = names
            hx = []
            if scaled:
                group([na, nv, na], [H1] * 3, [h] * 3)
            for half in range(2):
                ready = []
                for jj in range(HC):
                    j, i = half * HC + jj, jj % 2
                    ba, ma = tile(na, H1, h, middle=None if scaled else later)
                    if conv is not None:
                        cw = [col("ffn_conv_w", conv * 66 + q * 22 + j) for q in range(3)]
                        y = act(Y[i][:, :], PS[ba][:, :], ACT.Identity, scale=cw[2],
                                bias=col("ffn_conv_b", conv * 22 + j), w=(ma, gt[i]))
                        y = stt(Y[i][:, 1:512], PS[ba][:, 0:511], cw[1], Y[i][:, 1:512], ALU.mult, ALU.add, w=(y,))
                        y = stt(Y[i][:, 2:512], PS[ba][:, 0:510], cw[0], Y[i][:, 2:512], ALU.mult, ALU.add, w=(y,))
                        free[ba] = y
                        si = act(SI[i][:, :], Y[i][:, :], ACT.Silu, w=(y,))
                    else:
                        si = free[ba] = tt(SI[i][:, :], PS[ba][:, :], SG[:, :], ALU.mult, w=(ma, gt[i], factor[0]))
                        si = act(SI[i][:, :], SI[i][:, :], ACT.Silu, w=(si,))
                        si = tt(SI[i][:, :], SI[i][:, :], SG[:, :], ALU.mult, w=(si, factor[0]), e=PO)
                    bv, mv = tile(nv, H1, h)
                    g = free[bv] = tt(SI[i][:, :], SI[i][:, :], PS[bv][:, :], ALU.mult, w=(mv, si))
                    g1 = act(chunk(GH, jj), SI[i][:, :], w=(g, gfree))
                    g2 = tt(chunk(GL, jj), SI[i][:, :], chunk(GH, jj).bitcast(F32), ALU.subtract, w=(g1,))
                    gt[i] = g2
                    ready.append(g2)
                if half:
                    table("natural_log_exp")
                    hfree = PE.last()
                for n in range(8):
                    bk, m = tile(nd, (GH, GL), ready)
                    gfree = m
                    t = residual(n, b, m, bk, None if gate is None else MOD[:, gate + n:gate + n + 1],
                                 square=half == 1, second=second)
                    if half and last and n in (2, 5):
                        gained[n] = act(xk(n), xk(n), scale=col("final_g_2", n), w=(t,))
                    if half and gain is not None:
                        hx.append(split_x(n, gain, (t, hfree)))
            return hx

        ta = gains(8, "norm2_g", 0, 32)
        prepare(cur[0] + 2)
        r = norm_r(nb)
        (h,) = norm_apply(nb, r, [(H1H, H1L, AB[:, 8:16], mod(24), plain)], w=(ta, PE.last()))
        table("silu")
        ffn("a", nb, early, ("ffn_w_up", "ffn_w_up", "ffn_w_down"), h, 0, 40)
        usepool[0] = False
        ta1 = gains(16, "norm1_g", 8, 48 + 8)
        takv = gains(24, "kv_norm_g", 0, 96 + 8)
        gains(32, "norm2_g", 8, 48 + 32)
        prepare(cur[0] + 2)
        r = norm_r(nb, SG[:, :])
        early.close()
        barrier()

        att = ExitStack()
        H2H, H2L = sbuf("H2Hb", 4096, F32R, att), sbuf("H2Lb", 4096, F32R, att)
        H2 = (H2H, H2L)
        ATT = sbuf("ATT", 1152, F32, att)
        QT = [sbuf(f"QT{i}", 1536, F32, att) for i in range(2)]
        KT = [sbuf(f"KT{i}", 1536, F32, att) for i in range(2)]
        VV = [sbuf(f"VV{i}", 1536, F32, att) for i in range(2)]
        OT = sbuf("OT", 4096, F32, att)
        VF = sbuf("VF", 512, F32, att)
        STAT = sbuf("STAT", 16, F32, att)
        sub = ExitStack()
        nb = norm_bufs(sub, "b")
        nb["R"] = SG
        hq, hkv = norm_apply(nb, r, [(H1H, H1L, AB[:, 16:24], mod(48), permuted),
                                     (H2H, H2L, AB[:, 24:32], mod(96), permuted)], w=(ta1, takv, PE.last()))
        SP.wait(PE.last(), DVE.last(), SC.last(), PO.last())
        atok = s_att.sig(nc.sync.dma_start(ATT[:, :], attd))
        subtok = [DVE.last(), SC.last(), PO.last()]
        sub.close()
        SB = [sbuf(f"SB{i}", 1536, F32, att) for i in range(2)]
        PT = [sbuf(f"PT{i}", 1536, F32, att) for i in range(2)]

        used, vtok, defer = {}, [None], []
        qktok, vvtok = {}, {}
        group(["w_kv", "attn_w_q", "w_kv"], [H2, H1, H2], [hkv, hq, hkv], banks=(2, 3, 4))

        def project(t):
            p, x = t // 9, t % 9
            i = p % 2
            name, g, what = PAIR_TILES[x]

            def middle(k):
                while defer and k == 2:
                    defer.pop(0)()
                run_events(t + k / 8)

            bk, m = tile(name, H1 if what == "q" else H2, banks=(0, 1), middle=middle)
            if what == "v":
                tv = free[bk] = act(VF[:, :], PS[bk][:, :], w=(m, vtok[0]))

                def rest():
                    m2 = vtok[0] = turn4(5, [VF[:, 128 * q:128 * q + 128] for q in range(4)], (tv,))
                    vvtok[p] = free[5] = act(chunk(VV[i], g), PS[5][:, :], w=(m2, used.get(p - 2)))
                defer.append(rest)
            else:
                dst = (QT if what == "q" else KT)[i]
                qktok[p] = free[bk] = act(chunk(dst, g), PS[bk][:, :], scale=0.125 if what == "q" else 1.0,
                                           w=(m, used.get(p - 2)))

        sbfree, ptfree = [subtok, subtok], [subtok, subtok]
        stok, ttok, otok = {}, {}, {}

        def scores(p, r_):
            i, n = p % 2, (4 * p + r_) % 2
            sb = SB[n]
            tok = []
            for hh in range(2):
                po = slice(64 * hh, 64 * hh + 64)
                q = [QT[i][po, 512 * g + 128 * r_:512 * g + 128 * r_ + 128] for g in range(3)]
                m0 = mms([(PS[2 + hh][:, :], q[0], KT[i][po, 0:512], True, True)], w=(free[2 + hh], qktok[p]))
                m1 = mms([(PS[4][:, 256 * hh + 128 * g - 128:256 * hh + 128 * g], q[g],
                           KT[i][po, 512 * g + 128 * r_:512 * g + 128 * r_ + 128], hh == 0 and g == 1, True)
                          for g in (1, 2)], w=(free[4],) if hh == 0 else (tok[0][1],))
                tok.append((m0, m1))
            for hh in range(2):
                head = 2 * p + hh
                m0, m1 = tok[hh]
                o = 768 * hh
                free[2 + hh] = stt(sb[:, o:o + 512], ATT[:, 128 * (3 - r_):128 * (3 - r_) + 512],
                                   float(SL[0][head]), PS[2 + hh][:, :], ALU.mult, ALU.add,
                                   w=(m0, sbfree[n], atok))
                DVE.wait(tok[1][1])
                for g in (1, 2):
                    t1 = stt(sb[:, o + 384 + 128 * g:o + 512 + 128 * g], ATT[:, 768 + 128 * g:896 + 128 * g],
                             float(SL[g][head]), PS[4][:, 256 * hh + 128 * g - 128:256 * hh + 128 * g],
                             ALU.mult, ALU.add)
                z = 8 * n + 4 * hh
                DVE.wait(t1)
                t2 = DVE.sig(nc.vector.tensor_reduce(STAT[:, z:z + 1], sb[:, o:o + 768], AX_X, ALU.max))
                t3 = ts(STAT[:, z + 1:z + 2], STAT[:, z:z + 1], -1.0, None, ALU.mult, w=(t2,))
                stok[(p, r_, hh)] = act(sb[:, o:o + 768], sb[:, o:o + 768], ACT.Exp, bias=STAT[:, z + 1:z + 2],
                                        scale=1.0, accum_out=STAT[:, z + 2:z + 3], w=(t3,))
            free[4] = t1

        def norms(p, r_):
            n = (4 * p + r_) % 2
            for hh in range(2):
                z, o = 8 * n + 4 * hh, 768 * hh
                DVE.wait(stok[(p, r_, hh)])
                t = DVE.sig(nc.vector.reciprocal(STAT[:, z + 3:z + 4], STAT[:, z + 2:z + 3]))
                stok[(p, r_, hh)] = ts(SB[n][:, o:o + 768], SB[n][:, o:o + 768], STAT[:, z + 3:z + 4], None,
                                       ALU.mult, w=(t,))

        def transposes(p, r_):
            n = (4 * p + r_) % 2
            sb, pt = SB[n], PT[n]
            got = ttok[(p, r_)] = []

            def third(c):
                bk = 6 + (3 * (4 * p + r_) + c) % 2 if p < 7 else (7, 2, 3)[c]
                m = turn4(bk, [sb[:, 512 * c + 128 * q:512 * c + 128 * q + 128] for q in range(4)],
                          (stok[(p, r_, 0)], stok[(p, r_, 1)]))
                if c == 1:
                    DVE.wait(m, ptfree[n])
                    t = DVE.sig(nc.vector.tensor_copy(chunk(pt, c), PS[bk][:, :]))
                else:
                    t = act(chunk(pt, c), PS[bk][:, :], w=(m, ptfree[n]))
                free[bk] = t
                got.append(t)
                sbfree[n] = m

            third(0)
            third(1)
            if p < 7:
                defer.append(lambda: third(2))
            else:
                third(2)

        def values(p, r_):
            i, n = p % 2, (4 * p + r_) % 2
            pt = PT[n]
            PE.wait(ttok[(p, r_)], vvtok[p], free[5])
            for c in range(6):
                g, kt = (0, c) if c < 4 else (c - 3, r_)
                for hh in range(2):
                    v = VV[i][:, 512 * g + 128 * kt + 64 * hh:512 * g + 128 * kt + 64 * hh + 64]
                    ins = nc.tensor.matmul(PS[5][64 * hh:64 * hh + 64, 0:128], v,
                                           pt[:, 768 * hh + 128 * c:768 * hh + 128 * c + 128],
                                           start=c == 0, stop=c == 5, skip_group_check=True)
            m = ptfree[n] = PE.sig(ins)
            if r_ == 3:
                used[p] = m
            free[5] = otok[p] = act(OT[:, 512 * p + 128 * r_:512 * p + 128 * r_ + 128], PS[5][:, 0:128], w=(m,))

        events = []
        for g in range(32):
            at = 9 * (g // 4 + 1) - 2 + (0, 2, 4, 7)[g % 4]
            events += [(at + 0.25, g, scores), (at + 1.5, g, norms), (at + 2, g, transposes), (at + 3, g, values)]
        events.sort(key=lambda e: (e[0], e[1]))

        def run_events(until):
            while events and events[0][0] <= until + 0.1:
                _, g, fn = events.pop(0)
                fn(g // 4, g % 4)

        oready = [None] * 8

        def natural(ap):
            return ap.rearrange("p (j r) -> p j r", r=4)

        def out_split(k, e):
            src = chunk(OT, k).rearrange("p (r j) -> p j r", r=4)
            t = act(natural(chunk(H1H, k)), src, w=(otok[k], hfree))
            oready[k] = tt(natural(chunk(H1L, k)), src, natural(chunk(H1H, k).bitcast(F32)), ALU.subtract,
                           w=(t, otok[k], hfree), e=e)

        for t in range(72):
            run_events(t)
            project(t)
            if t == 68:
                hfree = PE.last()
            if t >= 69:
                out_split(2 * (t - 69), PO)
                out_split(2 * (t - 69) + 1, DVE)
        run_events(72)
        while defer:
            defer.pop(0)()
        out_split(6, PO)
        prepare(cur[0] + 2)
        run_events(72.3)

        steps = [(0, values), None, None, None, None, (1, norms), None, (1, transposes), (2, scores), (1, values),
                 None, None, None, (2, norms), None, (2, transposes), (3, scores), (2, values), None, None,
                 (3, norms), (3, transposes), (3, values)]

        def hook():
            step = steps.pop(0)
            if step is not None:
                step[1](7, step[0])

        def last_hook():
            while steps:
                hook()
            out_split(7, DVE)

        group(["attn_w_o"] * 3, [H1] * 3, [oready] * 3, split=7, hooks=[(n, hook if n < 20 else last_hook) for n in range(21)],
              banks=(0, 1, 6))
        barrier()
        att.close()

        lay = ExitStack()
        nb = norm_bufs(top, "q", True)
        nb.update(norm_bufs(lay, "c", more=True))
        for n in range(8):
            bk, m = tile("attn_w_o", H1, oready, banks=(2, 3, 4, 5, 7))
            residual(n, nb, m, bk, MOD[:, 64 + n:65 + n])
        prepare(cur[0] + 2)
        r = norm_r(nb)
        (h,) = norm_apply(nb, r, [(H1H, H1L, AB[:, 32:40], mod(48 + 24), plain)], w=(PE.last(),))
        table("silu")
        tg = tt(AB[:, 0:8], cols("final_g", 0, 8), cols("norm1_g_2", 0, 8), ALU.mult)
        SC.wait(tg)
        DVE.wait(tg)
        hx = ffn("b", nb, lay, ("ffn_w_up", "ffn_w_up", "ffn_w_down"), h, 1, 48 + 40, second=True, gain=AB[:, 0:8])
        prepare(cur[0] + 2)

        def both():
            r = norm_r(nb, SS[:, :], i=7)
            m = mms([(PS[6][:, :], ONES, SG[:, :], True, True)], w=(sga[0], free[6]))
            T0 = nb["SQ"][0]
            t = free[6] = tt(T0[:, :], SS[:, :], PS[6][:, :], ALU.mult, w=(r, m, nb["sq"][0]))
            t = tt(T0[:, :], T0[:, :], SS[:, :], ALU.mult, w=(t,))
            t = act(T0[:, :], T0[:, :], ACT.Ln, bias=EPSC, scale=1.0 / D, w=(t,))
            t = act(T0[:, :], T0[:, :], ACT.Exp, scale=-0.5, w=(t,))
            factor[0] = nb["sq"][0] = tt(SG[:, :], T0[:, :], SS[:, :], ALU.mult, w=(t, m, r))

        def single():
            factor[0] = norm_r(nb, SG[:, :], (DVE.last(), PO.last()), 7)

        late.append(both)
        barrier()
        lay.close()

        for l in range(2):
            lay = ExitStack()
            H2H, H2L = sbuf(f"H2Hc{l}", 4096, F32R, lay), sbuf(f"H2Lc{l}", 4096, F32R, lay)
            H2 = (H2H, H2L)
            RT = sbuf(f"RT{l}", 3072, F32, lay)
            DEC = [RT[:, 512 * i:512 * i + 512] for i in range(4)]
            COS, SIN = RT[:, 2048:2560], RT[:, 2560:3072]
            Q = [sbuf(f"Q{l}{i}", 512, F32, lay) for i in range(3)]
            K = [sbuf(f"K{l}{i}", 512, F32, lay) for i in range(3)]
            G = [sbuf(f"G{l}{i}", 512, F32, lay) for i in range(2)]
            W = [sbuf(f"W{l}{i}", 512, F32, lay) for i in range(3)]
            VR = sbuf(f"VR{l}", 512, F32, lay)
            TMP = [sbuf(f"TMP{l}{i}", 512, F32, lay) for i in range(2)]
            AA = sbuf(f"AA{l}", 1280, F32, lay)
            SPL = sbuf(f"SPL{l}", 1280, F32, lay)
            SPH, SPO = sbuf(f"SPH{l}", 1280, F32R, lay), sbuf(f"SPO{l}", 1280, F32R, lay)
            KR = sbuf(f"KR{l}", 256, F32R, lay)
            krtok = act(KR[:, :], BAS[:, 128:384])
            UNEGR, NONESR = KR[:, 0:128], KR[:, 128:256]
            OBS = [sbuf(f"OB{l}{i}", 512, F32, lay) for i in range(2)]
            OCS = [sbuf(f"OC{l}{i}", 512, F32, lay) for i in range(2)]
            SP.wait(PE.last(), DVE.last(), SC.last(), PO.last())
            rtok = s_ret.sig(nc.sync.dma_start(RT[:, :], retd))
            tok = {}
            tmpfree = {"k": None, "q": None}
            OFF = [0, 512, 896, 1152]
            WID = [512, 384, 256, 128]
            SBK = [(2, 0), (3, 0), (4, 0), (3, 384)]
            LBK = [(5, 0), (6, 0), (7, 0), (6, 384)]
            mixed = [None] * 8
            defer = []
            jobs = [(n, what) for n in range(8) for what, _ in HEAD_TILES[HEADS[n][0]]]

            def proj(t_):
                n, what = jobs[t_]
                kind, x = HEADS[n]
                i = n % 3
                done = tok.get(("used", n - 3))

                def middle(k_):
                    later(k_)
                    while defer and k_ == 2:
                        defer.pop(0)()
                    run_ev(t_ + k_ / 8)

                bk, m = tile("w_in_2", H1, hx, banks=(0, 1), middle=middle)
                if what in "kq" and kind == "r":
                    dst = (K if what == "k" else Q)[i]
                    tp = TMP[0 if what == "k" else 1]
                    s1 = act(tp[0:64, :], PS[bk][64:128, :], w=(m, tmpfree[what]))
                    s2 = act(tp[64:128, :], PS[bk][0:64, :])
                    c1 = free[bk] = tt(dst[:, :], PS[bk][:, :], COS, ALU.mult, w=(s2, done, turned))
                    c2 = tt(tp[:, :], tp[:, :], SIN, ALU.mult, w=(s1, s2, turned), e=PO)
                    t = tmpfree[what] = tt(dst[:, :], dst[:, :], tp[:, :], ALU.add, w=(c1, c2), e=PO)
                elif what in "kq":
                    dst = (K if what == "k" else Q)[i]
                    t = free[bk] = stt(dst[:, :], PS[bk][:, :], 1.0 if what == "k" else 128.0 ** -0.5, SG[:, :],
                                       ALU.mult, ALU.mult, w=(m, done, factor[0]))
                elif what == "g":
                    t = free[bk] = tt(G[x % 2][:, :], PS[bk][:, :], SG[:, :], ALU.mult,
                                      w=(m, tok.get(("gfree", x % 2)), factor[0]))
                    tok[("g", n)] = t
                else:
                    tv = free[bk] = tt(VR[:, :], PS[bk][:, :], SG[:, :], ALU.mult, w=(m, tok.get("vr"), factor[0]))

                    def rest():
                        m2 = tok["vr"] = turn4(7, [VR[:, 128 * q:128 * q + 128] for q in range(4)], (tv,))
                        tok[("v", n)] = free[7] = act(W[i][:, :], PS[7][:, :], w=(m2, done))
                    defer.append(rest)
                    t = None
                tok.setdefault(n, []).append(t)

            def products(n):
                i = n % 3
                for x in range(4):
                    b_, c0 = SBK[x]
                    m = mms([(PS[b_][:, c0:c0 + WID[x]], K[i][:, 128 * x:128 * x + 128],
                              Q[i][:, 128 * x:512], c0 == 0, True)], w=(free[b_], tok[n]))
                    tok[("z", x)] = m
                return m

            def weighted(n, ready, bk):
                i = n % 3
                its = [(PS[bk][:, 128 * x:512], W[i][:, 128 * x:128 * x + 128], AA[:, OFF[x]:OFF[x] + WID[x]],
                        x == 0, x == 3, ready[x]) for x in range(4)]
                m = mms(its, w=(free[bk], tok[("v", n)]))
                tok["aa"] = tok[("used", n)] = m
                return m

            def r1(n):
                products(n)
                ready = []
                for y in range(4):
                    b_, c0 = SBK[y]
                    t = tt(AA[:, OFF[y]:OFF[y] + WID[y]], PS[b_][:, c0:c0 + WID[y]],
                           DEC[HEADS[n][1]][:, 0:WID[y]], ALU.mult, w=(tok[("z", 3)], rtok, tok.get("aa")))
                    free[b_] = t
                    ready.append(t)
                tok[("rd", n)] = ready

            def r2(n):
                m = weighted(n, tok[("rd", n)], 5)
                tok[("o", n)] = free[5] = act(OBS[1][:, :], PS[5][:, :], w=(m, tok.get("ob1")))

            def r3(n):
                OB, OC = OBS[1], OCS[1]
                m = mms([(PS[6][:, :], ONES, OB[:, :], True, True)], w=(tok[("o", n)], free[6]))
                t = free[6] = stt(OB[:, :], PS[6][:, :], -1.0 / 128, OB[:, :], ALU.mult, ALU.add,
                                  w=(m, tok[("o", n)]))
                tok[("q", n)] = act(OC[:, :], OB[:, :], ACT.Square, w=(t, tok.get("oc1")))

            def s1(n):
                products(n)
                parts, ts_ = [], []
                for y in range(4):
                    b_, c0 = SBK[y]
                    a_ = AA[:, OFF[y]:OFF[y] + WID[y]]
                    ts_.append(act(a_, PS[b_][:, c0:c0 + WID[y]], ACT.Abs, w=(tok[("z", 3)], tok.get("aa"))))
                zt = ts_[3]
                masked = []
                for y in range(4):
                    b_, c0 = SBK[y]
                    z = PS[b_][:, c0:c0 + WID[y]]
                    a_ = AA[:, OFF[y]:OFF[y] + WID[y]]
                    s_ = SPL[:, OFF[y]:OFF[y] + WID[y]]
                    t = act(a_, a_, ACT.Exp, scale=-1.0, w=(ts_[y],))
                    t = act(a_, a_, ACT.Ln, bias=ONE, w=(t, kontok))
                    t = stt(s_, z, 0.0, a_, ALU.max, ALU.add, w=(t, zt, tok.get("sp")))
                    t = free[b_] = tt(a_, z, s_, ALU.subtract, w=(t,))
                    t = tt(s_[:, 0:128], s_[:, 0:128], STRICT, ALU.mult, w=(t,))
                    masked.append(t)
                for y in range(4):
                    h_, s_ = (b_[:, OFF[y]:OFF[y] + WID[y]] for b_ in (SPH, SPL))
                    t = act(h_, s_, w=(masked[y], tok.get("sp")))
                    t = tt(SPO[:, OFF[y]:OFF[y] + WID[y]], s_, h_.bitcast(F32), ALU.subtract, w=(t, tok.get("sp")))
                    parts.append(t)
                tok[("parts", n)] = parts

            def s2(n):
                parts = tok[("parts", n)]
                ready = []
                ms = []
                for y in (3, 2, 1, 0):
                    b_, c0 = LBK[y]
                    its = []
                    for j in range(y, 4):
                        for h_ in (SPH, SPO):
                            its.append((PS[b_][:, c0 + 128 * (j - y):c0 + WID[y]], UNEGR if j == y else NONESR,
                                        h_[:, OFF[j]:OFF[j] + WID[j]], j == y and y != 1 and h_ is SPH, j == 3,
                                        parts[j]))
                    ms.append(mms(its, w=(free[b_], krtok)))
                tok["sp"] = ms[3]
                ms = ms[::-1]
                for y in (3, 2, 1, 0):
                    b_, c0 = LBK[y]
                    a_ = AA[:, OFF[y]:OFF[y] + WID[y]]
                    t = free[b_] = tt(a_, a_, PS[b_][:, c0:c0 + WID[y]], ALU.add,
                                      w=(ms[1] if y == 3 else ms[y], parts[y]))
                    t = act(a_, a_, ACT.Exp, w=(t,))
                    ready.append(tt(a_[:, 0:128], a_[:, 0:128], STRICT, ALU.mult, w=(t,)))
                tok[("rd", n)] = ready[::-1]

            def s3(n):
                m = weighted(n, tok[("rd", n)], 2)
                tok[("o", n)] = t = free[2] = act(OBS[0][:, :], PS[2][:, :], w=(m, tok.get("ob0")))
                tok[("q", n)] = act(OCS[0][:, :], OBS[0][:, :], ACT.Square, w=(t, tok.get("oc0")))

            def finish(n):
                kind, x = HEADS[n]
                k = x if kind == "r" else 4 + x
                i = 1 if kind == "r" else 0
                OB, OC, bk = OBS[i], OCS[i], 6 if kind == "r" else 7
                m = mms([(PS[bk][:, :], ONES, OC[:, :], True, True)], w=(tok[("q", n)], free[bk]))
                q1 = free[bk] = act(OC[:, :], PS[bk][:, :], ACT.Ln, bias=EPSC, scale=1.0 / 128, w=(m,))
                q2 = act(OC[:, :], OC[:, :], ACT.Exp, scale=-0.5, w=(q1,))
                gc = col("ret_norm_g_2" if kind == "r" else "sb_norm_g_2", 4 * l + x)
                y1 = stt(OB[:, :], OB[:, :], gc, OC[:, :], ALU.mult, ALU.mult, w=(q2, tok[("o", n)], tok[("q", n)]))
                tok[f"oc{i}"] = y1
                if kind == "r":
                    y1 = tt(OB[:, :], OB[:, :], G[x % 2][:, :], ALU.mult, w=(y1, tok[("gs", n)]))
                    tok[("gfree", x % 2)] = y1
                y2 = act(chunk(H2H, k), OB[:, :], w=(y1,))
                y3 = tt(chunk(H2L, k), OB[:, :], chunk(H2H, k).bitcast(F32), ALU.subtract, w=(y2,))
                tok[f"ob{i}"] = mixed[k] = y3

            def gate_silu(n):
                table("silu")
                g = G[HEADS[n][1] % 2]
                tok[("gs", n)] = act(g[:, :], g[:, :], ACT.Silu, w=(tok[("g", n)],))
                table("natural_log_exp")

            events = []
            for x in range(4):
                a, b = 7 * x + 3, 7 * x + 7
                events += [(a + 1, 2 * x, s1), (a + 3, 2 * x, s2), (a + 4, 2 * x, s3), (a + 5, 2 * x, finish),
                           (b + 0.5, 2 * x + 1, r1), (b + 0.6, 2 * x + 1, gate_silu), (b + 1.5, 2 * x + 1, r2),
                           (b + 2.5, 2 * x + 1, r3), (b + 3.5, 2 * x + 1, finish)]
            events.sort(key=lambda e: (e[0], e[1]))

            def run_ev(until, events=events):
                while events and events[0][0] <= until:
                    _, n, fn = events.pop(0)
                    fn(n)

            for t_ in range(28):
                run_ev(t_)
                proj(t_)
                if t_ == 0:
                    t1 = tt(COS, COS, SG[:, :], ALU.mult, w=(rtok, factor[0]))
                    turned = tt(SIN, SIN, SG[:, :], ALU.mult, w=(t1,))
                if l == 0 and 1 <= t_ <= 8:
                    ssa[0] = stt(xk(t_ - 1), xk(t_ - 1), col("final_g", t_ - 1), SS[:, :], ALU.mult, ALU.mult,
                                 w=(hx,))
            while defer:
                defer.pop(0)()
            prepare(cur[0] + 2)
            run_ev(28.6)
            hfree = PE.last()
            order_ = (4, 0, 5, 1, 6, 2, 7, 3)
            hooks = {3: lambda: run_ev(29.9), 9: lambda: run_ev(30.5), 14: lambda: run_ev(1000)}
            group(["w_out_2"] * 3, [H2] * 3, [mixed] * 3, korder=order_, split=7, hooks=hooks.items(),
                  banks=(0, 1, 3))
            hx = []
            for n in range(8):
                bk, m = tile("w_out_2", H2, mixed, banks=(2, 4, 5, 6, 7))
                t = residual(n, nb, m, bk)
                hx.append(split_x(n, cols("norm2_g_2", 8 * l, 8), (t, hfree)))
            prepare(cur[0] + 2)
            late += [single, lambda: table("silu")]
            barrier()
            lay.close()
            lay = ExitStack()
            hx = ffn(f"d{l}", nb, lay, ("w_gate_2", "w_up_2", "w_down_2"), hx, None, None, scaled=False,
                     gain=None if l else cols("norm1_g_2", 8, 8), last=l == 1)
            prepare(cur[0] + 2)
            if l == 0:
                late.append(single)
            else:
                r = norm_r(nb, SG[:, :], (DVE.last(), PO.last()))
                for k in (0, 1, 3, 2, 4, 6, 7, 5):
                    if k in (2, 5):
                        t = tt(xk(k), xk(k), SG[:, :], ALU.mult, w=(r, gained[k]), e=PO)
                    else:
                        t = stt(xk(k), xk(k), col("final_g_2", k), SG[:, :], ALU.mult, ALU.mult, w=(r,))
                    SP.wait(t)
                    otk = s_out.sig(nc.sync.dma_start(out[128 * k:128 * k + 128, :], xk(k)))
            barrier()
            lay.close()
        SP.wait(otk, PE.last(), DVE.last(), SC.last(), PO.last())


def lay_out(inputs):
    parts = []
    for unit, _, tiles in plan():
        block = []
        for name, layer, k0, kn, n, nn in tiles:
            m = inputs[name] if layer is None else inputs[name][layer]
            if name == "pool_w_grp":
                m = m.reshape(1024, 256)
            b = m[128 * k0:128 * (k0 + kn), 128 * n:128 * (n + nn)]
            if unit == "ada":
                block.append(b.T)
            else:
                block.append(b.reshape(kn, 128, nn * 128).transpose(1, 0, 2).reshape(128, -1))
        parts.append(np.concatenate(block, axis=1).reshape(-1))
    stream = np.concatenate(parts)
    cols = np.concatenate([np.ascontiguousarray(inputs[n]).reshape(-1, 128).T for n, _ in COLS], axis=1)
    assert cols.shape == (128, NCOL)
    return stream, np.ascontiguousarray(inputs["c"][0]), np.ascontiguousarray(cols), np.ascontiguousarray(inputs["x"][0].T)


def kernel(**inputs):
    import concourse.bacc as _bacc
    from concourse.bass_utils import run_bass_kernel_spmd as _run

    ins = {k: np.asarray(v) for k, v in inputs.items()}
    stream, c, cols, xt = lay_out(ins)
    base, att, ret = tables()
    arrays = {"stream": stream, "c": c, "cols": cols, "xt": xt, "base": base, "att": att, "ret": ret}
    nc = _bacc.Bacc("TRN2", target_bir_lowering=False, num_devices=1, dynamic_dma_scratch_size=1024)
    args = [nc.dram_tensor(n, a.shape, F32, kind="ExternalInput").ap() for n, a in arrays.items()]
    y = nc.dram_tensor("y", (D, S), F32, kind="ExternalOutput").ap()
    program(nc, *args, y)
    r = _run(nc, [arrays], core_ids=[0])
    return np.ascontiguousarray(r.results[0]["y"].T).reshape(1, S, D)
```
